# Optimizing a Trainium2 kernel written in Bass

```python
import math
import jax, jax.numpy as jnp
from jax import lax
import numpy as np

D_MODEL = 1024
BATCH = 1
SEQ = 256
DEPTH = 1

CHUNK = 64
Q_BLOCK = 128
EPS = 1e-6

FOX_HEADS = 4
FOX_DIM = 128
GDN_HEADS = 4
GDN_DK = 128
GDN_DV = 128
GDN_CONV = 4
SB_HEADS = 4
SB_DIM = 128
MEM_TOKENS = 256
MEM_HEADS = 4
MEM_DIM = 128
D_FF = 2816
FFN_CONV = 3
N_BRANCH = 3

FOX_W = FOX_HEADS * FOX_DIM
GDN_KW = GDN_HEADS * GDN_DK
GDN_VW = GDN_HEADS * GDN_DV
SB_W = SB_HEADS * SB_DIM
MEM_W = MEM_HEADS * MEM_DIM

IN_SPLITS = (
    FOX_W, FOX_W, FOX_W, FOX_HEADS,
    GDN_KW, GDN_KW, GDN_VW, GDN_HEADS, GDN_HEADS, GDN_VW,
    SB_W, SB_W, SB_W,
    N_BRANCH * D_MODEL,
)
N_IN = sum(IN_SPLITS)


def rmsnorm(x, g):
    xf = x.astype(jnp.float32)
    y = xf * lax.rsqrt(jnp.mean(xf * xf, axis=-1, keepdims=True) + EPS)
    return (y * g.astype(jnp.float32)).astype(x.dtype)

def l2norm(x):
    xf = x.astype(jnp.float32)
    return xf * lax.rsqrt(jnp.sum(xf * xf, axis=-1, keepdims=True) + EPS)

def heads(x, n):
    return x.reshape(x.shape[:-1] + (n, -1))

def causal_dwconv(x, w):
    width, ch = w.shape
    return lax.conv_general_dilated(
        x, w[:, None, :].astype(x.dtype), window_strides=(1,), padding=[(width - 1, 0)],
        dimension_numbers=("NWC", "WIO", "NWC"), feature_group_count=ch)

def split_projection(p):
    points = [int(s) for s in np.cumsum(IN_SPLITS)[:-1]]
    return jnp.split(p, points, axis=-1)

def fox_attention(q, k, v, logf):
    B, S, H, dh = q.shape
    c = jnp.cumsum(logf, axis=1).transpose(0, 2, 1)
    qh = q.transpose(0, 2, 1, 3)
    kh = k.transpose(0, 2, 1, 3)
    vh = v.transpose(0, 2, 1, 3)
    scale = dh ** -0.5
    outs = []
    for i in range(S // Q_BLOCK):
        lo, hi = i * Q_BLOCK, (i + 1) * Q_BLOCK
        s = (jnp.einsum("bhqd,bhkd->bhqk", qh[:, :, lo:hi], kh[:, :, :hi]).astype(jnp.float32) * scale
             + (c[:, :, lo:hi, None] - c[:, :, None, :hi]))
        mask = jnp.arange(hi)[None, :] <= jnp.arange(lo, hi)[:, None]
        p = jax.nn.softmax(jnp.where(mask, s, -jnp.inf), axis=-1).astype(vh.dtype)
        outs.append(jnp.einsum("bhqk,bhkd->bhqd", p, vh[:, :, :hi]))
    o = jnp.concatenate(outs, axis=2)
    return o.transpose(0, 2, 1, 3).reshape(B, S, H * dh)

def stick_breaking_attention(q, k, v):
    B, S, H, dh = q.shape
    qh = q.transpose(0, 2, 1, 3)
    kh = k.transpose(0, 2, 1, 3)
    vh = v.transpose(0, 2, 1, 3)
    scale = dh ** -0.5
    idx = jnp.arange(Q_BLOCK)
    tri_in = (idx[:, None] >= idx[None, :]).astype(jnp.float32)
    outs = []
    for i in range(S // Q_BLOCK):
        lo, hi = i * Q_BLOCK, (i + 1) * Q_BLOCK
        nk = i + 1
        z = jnp.einsum("bhqd,bhkd->bhqk", qh[:, :, lo:hi], kh[:, :, :hi]).astype(jnp.float32) * scale
        mask = jnp.arange(hi)[None, :] < jnp.arange(lo, hi)[:, None]
        log_keep = jnp.where(mask, -jax.nn.softplus(z), 0.0)
        lk = log_keep.reshape(B, H, Q_BLOCK, nk, Q_BLOCK)
        within = jnp.einsum("bhqnj,jk->bhqnk", lk, tri_in)
        tot = jnp.sum(lk, axis=-1)
        blk = jnp.arange(nk)
        tri_blk = (blk[:, None] > blk[None, :]).astype(jnp.float32)
        after = jnp.einsum("bhqm,mn->bhqn", tot, tri_blk)
        rc = (within + after[..., None]).reshape(B, H, Q_BLOCK, hi)
        a = jnp.exp(jnp.where(mask, z + rc, -jnp.inf)).astype(vh.dtype)
        outs.append(jnp.einsum("bhqk,bhkd->bhqd", a, vh[:, :, :hi]))
    o = jnp.concatenate(outs, axis=2)
    return o.transpose(0, 2, 1, 3).reshape(B, S, H * dh)

def gated_delta_rule(q, k, v, g, beta):
    B, T, H, dk = q.shape
    dv = v.shape[-1]
    N = T // CHUNK
    f32 = jnp.float32

    def chunks(a):
        a = a.astype(f32).reshape((B, N, CHUNK, H) + a.shape[3:])
        return jnp.moveaxis(a, (1, 3), (0, 2))

    qc = chunks(q) * dk ** -0.5
    kc = chunks(k)
    vc = chunks(v)
    bc = chunks(beta)
    gc = jnp.cumsum(chunks(g), axis=-1)
    idx = jnp.arange(CHUNK)
    causal = idx[:, None] >= idx[None, :]
    strict = idx[:, None] > idx[None, :]
    decay = jnp.exp(jnp.where(causal, gc[..., :, None] - gc[..., None, :], -jnp.inf))
    kk = jnp.einsum("nbhcd,nbhed->nbhce", kc, kc)
    a_mat = jnp.where(strict, bc[..., :, None] * kk * decay, 0.0) + jnp.eye(CHUNK, dtype=f32)
    rhs = jnp.concatenate([vc * bc[..., None], kc * (bc * jnp.exp(gc))[..., None]], axis=-1)
    sol = lax.linalg.triangular_solve(a_mat, rhs, left_side=True, lower=True)
    u, w = sol[..., :dv], sol[..., dv:]
    attn = jnp.where(causal, jnp.einsum("nbhcd,nbhed->nbhce", qc, kc) * decay, 0.0)
    g_last = gc[..., -1]
    k_tail = kc * jnp.exp(g_last[..., None] - gc)[..., None]

    def step(state, xs):
        q_n, u_n, w_n, g_n, attn_n, kt_n, gl_n = xs
        v_new = u_n - jnp.einsum("bhck,bhkv->bhcv", w_n, state)
        o = (jnp.einsum("bhck,bhkv->bhcv", q_n * jnp.exp(g_n)[..., None], state)
             + jnp.einsum("bhce,bhev->bhcv", attn_n, v_new))
        state = state * jnp.exp(gl_n)[..., None, None] + jnp.einsum("bhck,bhcv->bhkv", kt_n, v_new)
        return state, o

    s0 = jnp.zeros((B, H, dk, dv), f32)
    _, o = lax.scan(step, s0, (qc, u, w, gc, attn, k_tail, g_last))
    return jnp.moveaxis(o, (0, 2), (1, 3)).reshape(B, T, H, dv)

def memory_cross_attention(h, m, w_q, w_kv, q_g, k_g, w_o):
    B, S, _ = h.shape
    q = rmsnorm(heads(h @ w_q, MEM_HEADS), q_g)
    k, v = jnp.split(m @ w_kv, 2, axis=-1)
    k = rmsnorm(heads(k, MEM_HEADS), k_g)
    v = heads(v, MEM_HEADS)
    s = jnp.einsum("bqhd,bkhd->bhqk", q, k).astype(jnp.float32) * MEM_DIM ** -0.5
    p = jax.nn.softmax(s, axis=-1).astype(v.dtype)
    o = jnp.einsum("bhqk,bkhd->bqhd", p, v).reshape(B, S, MEM_W)
    return o @ w_o

def conv_ffn(h, w_up, conv_w, conv_b, w_down):
    u = causal_dwconv(h @ w_up, conv_w) + conv_b
    a, b = jnp.split(u, 2, axis=-1)
    return (jax.nn.silu(a) * b) @ w_down

def first_inputs(seed: int = 0) -> dict:
    key = jax.random.key(seed)
    ks = iter(jax.random.split(key, 40))
    L, D = DEPTH, D_MODEL
    f32 = jnp.float32

    def nrm(shape, scale):
        return jax.random.normal(next(ks), shape, f32) * scale

    def gain(shape):
        return 1.0 + 0.02 * jax.random.normal(next(ks), shape, f32)

    x = nrm((BATCH, SEQ, D), 1.0)
    mem = nrm((BATCH, MEM_TOKENS, D), 1.0)
    norm_mix = gain((L, D))
    w_in = nrm((L, D, N_IN), D ** -0.5)
    fox_fbias = jax.random.uniform(next(ks), (L, FOX_HEADS), f32, minval=1.0, maxval=5.0)
    fox_qnorm = gain((L, FOX_DIM))
    fox_knorm = gain((L, FOX_DIM))
    gdn_conv = nrm((L, GDN_CONV, 2 * GDN_KW + GDN_VW), GDN_CONV ** -0.5)
    gdn_a_log = jnp.log(jax.random.uniform(next(ks), (L, GDN_HEADS), f32, minval=1.0, maxval=16.0))
    dt = jnp.exp(jax.random.uniform(next(ks), (L, GDN_HEADS), f32,
                                    minval=math.log(1e-3), maxval=math.log(1e-1)))
    gdn_dt_bias = dt + jnp.log(-jnp.expm1(-dt))
    gdn_onorm = gain((L, GDN_DV))
    gate_bias = nrm((L, N_BRANCH * D), 0.01)
    w_oa = nrm((L, FOX_W, D), FOX_W ** -0.5)
    w_ob = nrm((L, GDN_VW, D), GDN_VW ** -0.5)
    w_oc = nrm((L, SB_W, D), SB_W ** -0.5)
    w_out = nrm((L, D, D), D ** -0.5)
    norm_xq = gain((L, D))
    norm_mem = gain((L, D))
    w_mq = nrm((L, D, MEM_W), D ** -0.5)
    w_mkv = nrm((L, D, 2 * MEM_W), D ** -0.5)
    mq_norm = gain((L, MEM_DIM))
    mk_norm = gain((L, MEM_DIM))
    w_mo = nrm((L, MEM_W, D), MEM_W ** -0.5)
    norm_ffn = gain((L, D))
    w_up = nrm((L, D, 2 * D_FF), D ** -0.5)
    ffn_conv = nrm((L, FFN_CONV, 2 * D_FF), FFN_CONV ** -0.5)
    ffn_conv_b = nrm((L, 2 * D_FF), 0.01)
    w_down = nrm((L, D_FF, D), D_FF ** -0.5)
    return {
        "x": x, "mem": mem, "norm_mix": norm_mix, "w_in": w_in,
        "fox_fbias": fox_fbias, "fox_qnorm": fox_qnorm, "fox_knorm": fox_knorm,
        "gdn_conv": gdn_conv, "gdn_a_log": gdn_a_log, "gdn_dt_bias": gdn_dt_bias,
        "gdn_onorm": gdn_onorm, "gate_bias": gate_bias,
        "w_oa": w_oa, "w_ob": w_ob, "w_oc": w_oc, "w_out": w_out,
        "norm_xq": norm_xq, "norm_mem": norm_mem, "w_mq": w_mq, "w_mkv": w_mkv,
        "mq_norm": mq_norm, "mk_norm": mk_norm, "w_mo": w_mo,
        "norm_ffn": norm_ffn, "w_up": w_up, "ffn_conv": ffn_conv,
        "ffn_conv_b": ffn_conv_b, "w_down": w_down,
    }

def first_block(x, mem, norm_mix, w_in, fox_fbias, fox_qnorm, fox_knorm, gdn_conv, gdn_a_log,
              gdn_dt_bias, gdn_onorm, gate_bias, w_oa, w_ob, w_oc, w_out, norm_xq, norm_mem,
              w_mq, w_mkv, mq_norm, mk_norm, w_mo, norm_ffn, w_up, ffn_conv, ffn_conv_b, w_down):
    B, S, D = x.shape
    f32 = jnp.float32
    for l in range(DEPTH):
        h = rmsnorm(x, norm_mix[l])
        (fq, fk, fv, ff, gq, gk, gv, gb, ga, gz, sq, sk, sv, gates) = split_projection(h @ w_in[l])

        fq = rmsnorm(heads(fq, FOX_HEADS), fox_qnorm[l])
        fk = rmsnorm(heads(fk, FOX_HEADS), fox_knorm[l])
        logf = jax.nn.log_sigmoid((ff + fox_fbias[l]).astype(f32))
        ya = fox_attention(fq, fk, heads(fv, FOX_HEADS), logf)

        qkv = jax.nn.silu(causal_dwconv(jnp.concatenate([gq, gk, gv], axis=-1), gdn_conv[l]))
        cq, ck, cv = jnp.split(qkv, [GDN_KW, 2 * GDN_KW], axis=-1)
        beta = jax.nn.sigmoid(gb.astype(f32))
        g_log = -jnp.exp(gdn_a_log[l].astype(f32)) * jax.nn.softplus((ga + gdn_dt_bias[l]).astype(f32))
        o = gated_delta_rule(l2norm(heads(cq, GDN_HEADS)), l2norm(heads(ck, GDN_HEADS)),
                             heads(cv, GDN_HEADS), g_log, beta)
        yb = (rmsnorm(o, gdn_onorm[l]) * jax.nn.silu(heads(gz, GDN_HEADS).astype(f32)))
        yb = yb.astype(x.dtype).reshape(B, S, GDN_VW)

        yc = stick_breaking_attention(heads(sq, SB_HEADS), heads(sk, SB_HEADS), heads(sv, SB_HEADS))

        g = jax.nn.sigmoid((gates + gate_bias[l]).astype(f32)).astype(x.dtype).reshape(B, S, N_BRANCH, D)
        mixed = (g[..., 0, :] * (ya @ w_oa[l]) + g[..., 1, :] * (yb @ w_ob[l])
                 + g[..., 2, :] * (yc @ w_oc[l]))
        x = x + mixed @ w_out[l]

        x = x + memory_cross_attention(rmsnorm(x, norm_xq[l]), rmsnorm(mem, norm_mem[l]),
                                       w_mq[l], w_mkv[l], mq_norm[l], mk_norm[l], w_mo[l])

        x = x + conv_ffn(rmsnorm(x, norm_ffn[l]), w_up[l], ffn_conv[l], ffn_conv_b[l], w_down[l])
    return x


D_MIX = D_MODEL
N_ATTN_HEADS = 8
ATTN_HEAD_DIM = 64
D_ATTN = N_ATTN_HEADS * ATTN_HEAD_DIM
D_POOL = D_MIX - D_ATTN
POOL_WINDOWS = (2, 4, 8, 16)
N_POOL_GROUPS = len(POOL_WINDOWS)
POOL_GROUP_DIM = D_POOL // N_POOL_GROUPS
D_IN = 3 * D_ATTN + D_POOL
MOBA_BLOCK = 256
MOBA_TOPK = 3
Q_CHUNK = 32
N_MEM = 256
XA_HEADS = 4
XA_HEAD_DIM = D_MODEL // XA_HEADS
MACARON_WEIGHT = 0.5
RMS_EPS = 1e-6


def rmsnorm_2(x, g):
    xf = x.astype(jnp.float32)
    r = lax.rsqrt(jnp.mean(xf * xf, axis=-1, keepdims=True) + RMS_EPS)
    return (xf * r).astype(x.dtype) * g

def swiglu(h, w_gate, w_up, w_down):
    return (jax.nn.silu(h @ w_gate) * (h @ w_up)) @ w_down

def alibi_slopes(n_heads):
    s = 2.0 ** (-8.0 * np.arange(1, n_heads + 1) / n_heads)
    return jnp.asarray(s, dtype=jnp.float32)

def moba_attention(q, k, v, slopes):
    B, H, S, dh = q.shape
    L = MOBA_BLOCK
    s_pad = ((S + L - 1) // L) * L
    pad = s_pad - S
    kp = jnp.pad(k, ((0, 0), (0, 0), (0, pad), (0, 0)))
    vp = jnp.pad(v, ((0, 0), (0, 0), (0, pad), (0, 0)))
    nb = s_pad // L
    n_sel = min(MOBA_TOPK, nb)
    kb = kp.reshape(B, H, nb, L, dh)
    vb = vp.reshape(B, H, nb, L, dh)
    k_mean = jnp.mean(kb, axis=3)
    qs = q * (dh ** -0.5)
    bi = jnp.arange(B)[:, None, None, None]
    hi = jnp.arange(H)[None, :, None, None]
    lpos = jnp.arange(L)
    slot = jnp.arange(n_sel)
    blk_ids = jnp.arange(nb)
    n_chunks = S // Q_CHUNK

    def chunk(c):
        start = c * Q_CHUNK
        qc = lax.dynamic_slice_in_dim(qs, start, Q_CHUNK, axis=2)
        qpos = start + jnp.arange(Q_CHUNK)
        qpos_f = qpos.astype(jnp.float32)
        own = start // L
        gate = jnp.einsum('bhqd,bhnd->bhqn', qc, k_mean).astype(jnp.float32)
        gate = jnp.where(blk_ids < own, gate, -jnp.inf)
        _, idx = lax.top_k(gate, n_sel)
        slot_ok = slot < own
        k_sel = kb[bi, hi, idx]
        v_sel = vb[bi, hi, idx]
        kpos_sel = (idx[..., None] * L + lpos).astype(jnp.float32)
        s_sel = (jnp.einsum('bhqd,bhqrld->bhqrl', qc, k_sel).astype(jnp.float32)
                 - slopes[:, None, None, None] * (qpos_f[:, None, None] - kpos_sel))
        s_sel = jnp.where(slot_ok[:, None], s_sel, -jnp.inf)
        k_own = lax.dynamic_index_in_dim(kb, own, axis=2, keepdims=False)
        v_own = lax.dynamic_index_in_dim(vb, own, axis=2, keepdims=False)
        kpos_own = own * L + lpos
        s_own = (jnp.einsum('bhqd,bhld->bhql', qc, k_own).astype(jnp.float32)
                 - slopes[:, None, None] * (qpos_f[:, None] - kpos_own.astype(jnp.float32)[None, :]))
        s_own = jnp.where(kpos_own[None, :] <= qpos[:, None], s_own, -jnp.inf)
        scores = jnp.concatenate([s_sel.reshape(B, H, Q_CHUNK, n_sel * L), s_own], axis=-1)
        p = jax.nn.softmax(scores, axis=-1)
        p_sel = p[..., :n_sel * L].reshape(B, H, Q_CHUNK, n_sel, L).astype(v.dtype)
        p_own = p[..., n_sel * L:].astype(v.dtype)
        return (jnp.einsum('bhqrl,bhqrld->bhqd', p_sel, v_sel)
                + jnp.einsum('bhql,bhld->bhqd', p_own, v_own))

    outs = lax.map(chunk, jnp.arange(n_chunks))
    return outs.transpose(1, 2, 0, 3, 4).reshape(B, H, S, dh)

def multiscale_pool(p, pool_w, pool_scale):
    B, S, C = p.shape
    pf = p.reshape(B, S, N_POOL_GROUPS, POOL_GROUP_DIM).astype(jnp.float32)
    cs = jnp.concatenate([jnp.zeros((B, 1, N_POOL_GROUPS, POOL_GROUP_DIM), jnp.float32),
                          lax.cumsum(pf, axis=1)], axis=1)
    t = jnp.arange(S)
    outs = []
    for g, w in enumerate(POOL_WINDOWS):
        lo = jnp.maximum(t + 1 - w, 0)
        cnt = (t + 1 - lo).astype(jnp.float32)
        mean = (cs[:, 1:, g] - cs[:, lo, g]) / cnt[None, :, None]
        outs.append(mean - pf[:, :, g])
    d = jnp.stack(outs, axis=2).astype(p.dtype)
    y = jnp.einsum('bsgc,gcd->bsgd', d, pool_w)
    return y.reshape(B, S, C) * pool_scale

def memory_cross_attention_2(h, mem_n, wq, wkv, wo):
    B, S, _ = h.shape
    M = mem_n.shape[1]
    q = (h @ wq).reshape(B, S, XA_HEADS, XA_HEAD_DIM)
    kv = mem_n @ wkv
    k = kv[..., :D_MODEL].reshape(B, M, XA_HEADS, XA_HEAD_DIM)
    v = kv[..., D_MODEL:].reshape(B, M, XA_HEADS, XA_HEAD_DIM)
    s = jnp.einsum('bshd,bmhd->bhsm', q, k).astype(jnp.float32) * (XA_HEAD_DIM ** -0.5)
    p = jax.nn.softmax(s, axis=-1).astype(v.dtype)
    o = jnp.einsum('bhsm,bmhd->bshd', p, v).reshape(B, S, XA_HEADS * XA_HEAD_DIM)
    return o @ wo

def second_inputs(seed: int = 0) -> dict:
    key = jax.random.key(seed)
    ks = jax.random.split(key, 24)

    def nrm(k, shape, fan_in):
        return jax.random.normal(k, shape, jnp.float32) * fan_in ** -0.5

    def gain(k, shape):
        return 1.0 + 0.1 * jax.random.normal(k, shape, jnp.float32)

    L = DEPTH
    return {
        "x": jax.random.normal(ks[0], (BATCH, SEQ, D_MODEL), jnp.float32),
        "mem": jax.random.normal(ks[1], (BATCH, N_MEM, D_MODEL), jnp.float32),
        "ffn1_pre_g": gain(ks[2], (L, D_MODEL)),
        "ffn1_w_gate": nrm(ks[3], (L, D_MODEL, D_FF), D_MODEL),
        "ffn1_w_up": nrm(ks[4], (L, D_MODEL, D_FF), D_MODEL),
        "ffn1_w_down": nrm(ks[5], (L, D_FF, D_MODEL), D_FF),
        "ffn1_post_g": gain(ks[6], (L, D_MODEL)),
        "mix_pre_g": gain(ks[7], (L, D_MODEL)),
        "w_in": nrm(ks[8], (L, D_MODEL, D_IN), D_MODEL),
        "pool_w": nrm(ks[9], (L, N_POOL_GROUPS, POOL_GROUP_DIM, POOL_GROUP_DIM), POOL_GROUP_DIM),
        "pool_scale": gain(ks[10], (L, D_POOL)),
        "w_out": nrm(ks[11], (L, D_MIX, D_MODEL), D_MIX),
        "mix_post_g": gain(ks[12], (L, D_MODEL)),
        "xa_pre_g": gain(ks[13], (L, D_MODEL)),
        "mem_g": gain(ks[14], (L, D_MODEL)),
        "xa_wq": nrm(ks[15], (L, D_MODEL, XA_HEADS * XA_HEAD_DIM), D_MODEL),
        "xa_wkv": nrm(ks[16], (L, D_MODEL, 2 * XA_HEADS * XA_HEAD_DIM), D_MODEL),
        "xa_wo": nrm(ks[17], (L, XA_HEADS * XA_HEAD_DIM, D_MODEL), XA_HEADS * XA_HEAD_DIM),
        "xa_post_g": gain(ks[18], (L, D_MODEL)),
        "ffn2_pre_g": gain(ks[19], (L, D_MODEL)),
        "ffn2_w_gate": nrm(ks[20], (L, D_MODEL, D_FF), D_MODEL),
        "ffn2_w_up": nrm(ks[21], (L, D_MODEL, D_FF), D_MODEL),
        "ffn2_w_down": nrm(ks[22], (L, D_FF, D_MODEL), D_FF),
        "ffn2_post_g": gain(ks[23], (L, D_MODEL)),
    }

def second_block(x, mem, ffn1_pre_g, ffn1_w_gate, ffn1_w_up, ffn1_w_down, ffn1_post_g,
              mix_pre_g, w_in, pool_w, pool_scale, w_out, mix_post_g,
              xa_pre_g, mem_g, xa_wq, xa_wkv, xa_wo, xa_post_g,
              ffn2_pre_g, ffn2_w_gate, ffn2_w_up, ffn2_w_down, ffn2_post_g):
    B, S, _ = x.shape
    slopes = alibi_slopes(N_ATTN_HEADS)
    for l in range(DEPTH):
        h = rmsnorm_2(x, ffn1_pre_g[l])
        f = swiglu(h, ffn1_w_gate[l], ffn1_w_up[l], ffn1_w_down[l])
        x = x + MACARON_WEIGHT * rmsnorm_2(f, ffn1_post_g[l])

        h = rmsnorm_2(x, mix_pre_g[l])
        proj = h @ w_in[l]
        q = proj[..., :D_ATTN]
        k = proj[..., D_ATTN:2 * D_ATTN]
        v = proj[..., 2 * D_ATTN:3 * D_ATTN]
        p_in = proj[..., 3 * D_ATTN:]
        to_heads = lambda t: t.reshape(B, S, N_ATTN_HEADS, ATTN_HEAD_DIM).transpose(0, 2, 1, 3)
        attn = moba_attention(to_heads(q), to_heads(k), to_heads(v), slopes)
        attn = attn.transpose(0, 2, 1, 3).reshape(B, S, D_ATTN)
        pool = multiscale_pool(p_in, pool_w[l], pool_scale[l])
        y = jnp.concatenate([attn, pool], axis=-1) @ w_out[l]
        x = x + rmsnorm_2(y, mix_post_g[l])

        h = rmsnorm_2(x, xa_pre_g[l])
        mem_n = rmsnorm_2(mem, mem_g[l])
        c = memory_cross_attention_2(h, mem_n, xa_wq[l], xa_wkv[l], xa_wo[l])
        x = x + rmsnorm_2(c, xa_post_g[l])

        h = rmsnorm_2(x, ffn2_pre_g[l])
        f = swiglu(h, ffn2_w_gate[l], ffn2_w_up[l], ffn2_w_down[l])
        x = x + MACARON_WEIGHT * rmsnorm_2(f, ffn2_post_g[l])
    return x


def setup_inputs(seed=0):
    out = dict(first_inputs(seed))
    for name, value in second_inputs(seed + 1).items():
        if name != "x":
            out[name + "_2"] = value
    return out


def reference(
    x, mem, norm_mix, w_in, fox_fbias, fox_qnorm, fox_knorm, gdn_conv, gdn_a_log, gdn_dt_bias,
    gdn_onorm, gate_bias, w_oa, w_ob, w_oc, w_out, norm_xq, norm_mem, w_mq, w_mkv, mq_norm,
    mk_norm, w_mo, norm_ffn, w_up, ffn_conv, ffn_conv_b, w_down, mem_2, ffn1_pre_g_2,
    ffn1_w_gate_2, ffn1_w_up_2, ffn1_w_down_2, ffn1_post_g_2, mix_pre_g_2, w_in_2, pool_w_2,
    pool_scale_2, w_out_2, mix_post_g_2, xa_pre_g_2, mem_g_2, xa_wq_2, xa_wkv_2, xa_wo_2,
    xa_post_g_2, ffn2_pre_g_2, ffn2_w_gate_2, ffn2_w_up_2, ffn2_w_down_2, ffn2_post_g_2,
):
    x = first_block(
        x, mem, norm_mix, w_in, fox_fbias, fox_qnorm, fox_knorm, gdn_conv, gdn_a_log,
        gdn_dt_bias, gdn_onorm, gate_bias, w_oa, w_ob, w_oc, w_out, norm_xq, norm_mem, w_mq,
        w_mkv, mq_norm, mk_norm, w_mo, norm_ffn, w_up, ffn_conv, ffn_conv_b, w_down,
    )
    return second_block(
        x, mem_2, ffn1_pre_g_2, ffn1_w_gate_2, ffn1_w_up_2, ffn1_w_down_2, ffn1_post_g_2,
        mix_pre_g_2, w_in_2, pool_w_2, pool_scale_2, w_out_2, mix_post_g_2, xa_pre_g_2, mem_g_2,
        xa_wq_2, xa_wkv_2, xa_wo_2, xa_post_g_2, ffn2_pre_g_2, ffn2_w_gate_2, ffn2_w_up_2,
        ffn2_w_down_2, ffn2_post_g_2,
    )


_drawn_inputs = setup_inputs


def setup_inputs(seed=0):
    import zlib

    import numpy as np

    out = dict(_drawn_inputs(seed))
    spreads = {}
    factors = {'norm_mix': 3.277,
     'fox_qnorm': 8.0,
     'fox_knorm': 8.0,
     'gdn_onorm': 6.936,
     'gate_bias': 8.0,
     'norm_xq': 8.0,
     'norm_mem': 8.0,
     'mq_norm': 8.0,
     'mk_norm': 8.0,
     'norm_ffn': 12.602,
     'ffn_conv_b': 24.774,
     'ffn1_pre_g_2': 64.0,
     'ffn1_post_g_2': 64.0,
     'mix_pre_g_2': 48.081,
     'pool_scale_2': 56.432,
     'mix_post_g_2': 54.945,
     'xa_pre_g_2': 8.0,
     'mem_g_2': 6.633,
     'xa_post_g_2': 63.22,
     'ffn2_pre_g_2': 64.0,
     'ffn2_post_g_2': 64.0}
    for name, (base, spread) in spreads.items():
        noise = np.random.default_rng([zlib.crc32(name.encode()), seed]).standard_normal(out[name].shape)
        drawn = base * np.exp(spread * noise) if base else spread * noise
        out[name] = __import__('jax').numpy.asarray(drawn.astype(out[name].dtype))
    for name, factor in factors.items():
        out[name] = (out[name] * factor).astype(out[name].dtype)
    return out
```

```python
from contextlib import ExitStack

import numpy as np

import concourse.bass as bass
from concourse import mybir

F32 = mybir.dt.float32
F32R = mybir.dt.float32r
ALU = mybir.AluOpType
ACT = mybir.ActivationFunctionType
AX_X = mybir.AxisListType.X

P = 128
T = 256
NT = T // P
D = 1024
KD = D // P
HD = 128
NH = 4
DFF = 2816
KF = DFF // P
EPS = 1e-6
NEG = -1e30
CH = 64

RING = 3
LEAD = 2

FQ, FK, FV, FF = 0, 512, 1024, 1536
GQ = 1540
GB = GQ + 3 * 512
GA = GB + 4
GZ = GA + 4
SQ = GZ + 512
SK, SV = SQ + 512, SQ + 1024
GATES = SQ + 3 * 512


def param_columns():
    col, n = {}, 0
    for name, rows in [("norm_mix", 8), ("norm_xq", 8), ("norm_mem", 8), ("norm_ffn", 8), ("ffn1_pre_g_2", 8),
                       ("mix_pre_g_2", 8), ("xa_pre_g_2", 8), ("mem_g_2", 8), ("ffn2_pre_g_2", 8),
                       ("gdn_conv", 48), ("fox_qnorm", 1), ("fox_knorm", 1), ("gdn_onorm", 1),
                       ("mq_norm", 1), ("mk_norm", 1)]:
        col[name] = n
        n += rows
    first = n
    n = 128
    for name, rows in [("ffn_conv", 3 * 2 * KF), ("ffn_conv_b", 2 * KF), ("gate_bias", 24), ("pool_scale_2", 4)]:
        col[name] = n
        n += rows
    return col, first, n


class Plan:

    def __init__(self):
        self.steps, self.number, self.engine = [], {}, {}
        self.count = {"pe": 0, "act": 0, "dve": 0, "pool": 0}
        self.chunks, self.bank_read, self.bank_wait, self.ready = [], {}, {}, {}

    def add(self, engine, name, *args):
        self.count[engine] += 1
        self.steps.append((engine, name, args))
        self.number[(name, *args)] = self.count[engine]
        self.engine[name] = engine

    def take(self, user, banks, reader):
        self.bank_wait[user] = [r for r in dict.fromkeys(self.bank_read.get(b) for b in banks) if r]
        for b in banks:
            self.bank_read[b] = reader


def build_chunks(w):
    out = []

    def kpn(a):
        return a.rearrange("(k p) n -> p k n", p=P)

    def cols(name, c0, x, banks, evac, **k):
        out.append(dict(kind="A", srcs=[((0, 256), kpn(w[name][:, c0:c0 + 256]))], x=x, banks=banks, evac=evac, **k))

    def vals(name, c0, x, evac, **k):
        for half in range(2):
            out.append(dict(kind="V", half=half, srcs=[((0, 512), kpn(w[name][512 * half:512 * half + 512, c0:c0 + 512]))],
                            x=x, banks=(2, 3), evac=evac if half else None, **k))

    def rows(name, n, x, evac):
        for j in range(n):
            out.append(dict(kind="R", j=j, last=j == n - 1, srcs=[((0, 1024), kpn(w[name][256 * j:256 * j + 256, :]))],
                            x=x, banks=(4, 5, 6, 7), evac=evac if j == n - 1 else None, name=name))

    win = "w_in"
    out.append(dict(kind="S", srcs=[((0, 128), kpn(w[win][:, FF:FF + 128])), ((128, 256), kpn(w[win][:, GB:GB + 128]))],
                    x="x", banks=(0, 1), evac="rows"))
    turn = 1
    for i in range(6):
        cols(win, GQ + 256 * i, "x", (turn % 2,), "conv", i=i)
        turn += 1
    for what, c0 in (("fq", FQ), ("fk", FK)):
        for i in range(2):
            cols(win, c0 + 256 * i, "x", (turn % 2,), "copy", to=what, i=i)
            turn += 1
    vals(win, FV, "x", "vcopy", to="fv")
    for what, c0 in (("sq", SQ), ("sk", SK)):
        for i in range(2):
            cols(win, c0 + 256 * i, "x", (turn % 2,), "copy", to=what, i=i)
            turn += 1
    vals(win, SV, "x", "vcopy", to="sv")
    for i in range(2):
        cols(win, GZ + 256 * i, "x", (turn % 2,), "gz", i=i)
        turn += 1
    for i in range(12):
        cols(win, GATES + 256 * i, "x", (turn % 2,), "gate", i=i)
        turn += 1
    for br, name in ((2, "w_oc"), (0, "w_oa"), (1, "w_ob")):
        for i in range(2):
            out.append(dict(kind="O", srcs=[((0, 512), kpn(w[name][:, 512 * i:512 * i + 512]))], x="y%d" % br, br=br,
                            i=i, banks=(2 * i, 2 * i + 1), evac="gated"))
    rows("w_out", 4, "x", "resid")
    for i in range(2):
        cols("w_mkv", 256 * i, "m1", (i,), "copy", to="mk", i=i)
    vals("w_mkv", 512, "m1", "vcopy", to="mv")
    for i in range(2):
        cols("w_mq", 256 * i, "x", (i,), "copy", to="mq", i=i)
    rows("w_mo", 2, "ym", "resid")

    def ffn(f, gate, up, down, c_up):
        for i in range(KF // 2):
            cols(gate, 256 * i, "x", (2 * (i % 2),), None, f=f, i=i, part="gate")
            cols(up, c_up + 256 * i, "x", (2 * (i % 2) + 1,), "ffn", f=f, i=i, part="up")
        rows(down, KF // 2, "h%d" % f, "resid" if f == 0 else "post")

    ffn(0, "w_up", "w_up", "w_down", DFF)
    ffn(1, "ffn1_w_gate_2", "ffn1_w_up_2", "ffn1_w_down_2", 0)
    win = "w_in_2"
    for i in range(4):
        cols(win, 256 * i, "x", (i % 2,), "copy", to="qk", i=i)
    vals(win, 1024, "x", "vcopy", to="bv")
    for i in range(2):
        cols(win, 1536 + 256 * i, "x", (i % 2,), "copy", to="pin", i=i)
    for i in range(4):
        cols("xa_wkv_2", 256 * i, "m2", (i % 2,), "copy", to="xk", i=i)
    for i in range(2):
        vals("xa_wkv_2", 1024 + 512 * i, "m2", "vcopy", to="xv%d" % i)
    rows("w_out_2", 4, "y5", "post")
    for i in range(4):
        cols("xa_wq_2", 256 * i, "x", (i % 2,), "copy", to="xq", i=i)
    rows("xa_wo_2", 4, "y5", "post")
    ffn(2, "ffn2_w_gate_2", "ffn2_w_up_2", "ffn2_w_down_2", 0)
    for c in out:
        c.setdefault("name", "")
    return out


def build_plan(chunks):
    pl = Plan()
    pl.chunks = chunks
    n = len(chunks)
    side = []
    ready = {f"y{br}": [("yl", br)] for br in range(3)}
    ready["ym"] = [("ol", "mem", 2), ("ol", "mem", 3)]

    def hook(k=1):
        for chain in list(side):
            for _ in range(k):
                if chain:
                    for s in chain.pop(0):
                        place(s)
            if not chain:
                side.remove(chain)

    def place(s):
        if callable(s):
            s()
        else:
            pl.add(*s)

    def drain():
        while side:
            hook()

    def split(c):
        if c < n:
            pl.add("act", "hi", c)
            pl.add("dve", "lo", c)

    def mm(c, k=1):
        ch = chunks[c]
        pl.ready[c] = [("fl", int(ch["x"][1]), ch["j"])] if ch["x"][0] == "h" else ready[ch["x"]]
        split(c + LEAD)
        ev = ch["evac"]
        end = {"conv": ("cv_add", c), "copy": ("copy", c), "vcopy": ("copy", c), "gz": ("copy", c), "gate": ("copy", c),
               "rows": ("rows1",), "gated": ("gated", c), "resid": ("resid", c), "post": ("post2", c)}
        if ch["kind"] in "AOS":
            if "f" in ch:
                reader = ("cd", ch["i"]) if ch["f"] == 0 else ("fm" if ch["part"] == "up" else "fs", ch["f"], ch["i"])
            else:
                reader = end[ev]
            pl.take(("mm", c, 0), ch["banks"], reader)
        elif ch["kind"] == "V" and ch["half"] == 0:
            pl.take(("mm", c, 0), ch["banks"], ("copy", c + 1))
        elif ch["kind"] == "R" and ch["j"] == 0:
            e = c
            while not chunks[e]["last"]:
                e += 1
            pl.take(("mm", c, 0), ch["banks"], end[chunks[e]["evac"]][:1] + (e,))
        pl.add("pe", "mm", c, 0)
        hook(k)
        pl.add("pe", "mm", c, 1)
        if ev == "rows":
            for s in [("dve", "rows1"), ("act", "rows2"), ("dve", "rows3"), ("act", "rows4"), ("dve", "rows5"),
                      ("pe", "rows6"), ("dve", "rows7")]:
                pl.add(*s)
        elif ev == "conv":
            pl.add("act", "cv_mul", c)
            pl.add("dve", "cv_add", c)
            pl.add("act", "cv_silu", c)
        elif ev in ("copy", "vcopy", "gz", "gate"):
            pl.add("act", "copy", c)
        elif ev == "gated":
            pl.add("dve", "gated", c)
        elif ev == "resid":
            pl.add("dve", "resid", c)
        elif ev == "post":
            pl.add("dve", "post0", c)
            pl.add("act", "post1", c)
            pl.add("dve", "post2", c)
        elif ev == "ffn":
            f, i = ch["f"], ch["i"]
            if f == 0:
                pl.add("act", "ca", i)
                pl.add("dve", "cd", i)
            pl.add("act", "fs", f, i)
            pl.add("dve", "fm", f, i)
            pl.add("act", "fh", f, i)
            pl.add("dve", "fl", f, i)
        hook(k)

    def norm(name, into="x"):
        pl.add("dve", "ns", name)
        pl.add("act", "nr", name)
        pl.add("dve", "nd", name)
        for j in range(4):
            pl.take(("nt", name, j), (j,), ("nl", name, j))
            pl.add("pe", "nt", name, j)
            pl.add("act", "nh", name, j)
            pl.add("dve", "nl", name, j)

        ready[into] = [("nl", name, 3)]

    def hn(job):
        return [[("act", "hn_sq", job), ("pe", "hn_sum", job), ("act", "hn_r", job), ("dve", "hn_mul", job)]]

    def gdn(t):
        c = [[("pe", "g_dec", t), ("dve", "g_mask", t), ("act", "g_exp", t)],
             [("pe", "g_kk", t), ("dve", "g_m", t), ("pool", "g_eye", t)],
             [("pe", "g_turn", t), ("act", "g_kb", t), ("dve", "g_vb", t)]]
        for l in range(6):
            c += [[("pool", "l_mask", t, l), ("pe", "l_u", t, l), ("act", "l_uc", t, l)],
                  [("pe", "l_x", t, l), ("dve", "l_upd", t, l)]]
        c += [[("pe", "g_uw", t), ("dve", "g_u", t), ("act", "g_w", t)],
              [("pe", "g_bc", t), ("act", "g_egc", t), ("dve", "g_qg", t)]]
        for j in range(2):
            c += [[("pe", "r_ws", t, j), ("dve", "r_vn", t, j)],
                  [("pe", "r_o", t, j), ("act", "r_oc", t, j), ("dve", "r_s", t, j)]]
        return c

    def attend(kind, h):
        lane = kind, h
        return [[("pe", "sc", *lane), ("dve", "sm", *lane), ("act", "ex", *lane), ("dve", "pn", *lane)],
                [("pe", "pt", *lane), ("act", "pc", *lane)],
                [("pe", "pv", *lane), ("act", "oc", *lane)] + ([] if kind == "fox" else [("dve", "ol", *lane)])]

    def stick(h):
        return [[("pe", "z_s", h), ("act", "z_e", h), ("dve", "z_lk", h)],
                [("pe", "z_rc", h), ("dve", "z_w", h), ("act", "z_x", h)],
                [("pe", "z_o", h), ("act", "z_oc", h)]]

    pl.add("pool", "consts")
    pl.add("pe", "params")
    pl.add("dve", "params_c")
    split(0)
    split(1)
    norm("norm_mix")
    pl.add("pool", "consts2")
    c = 0
    for _ in range(7):
        mm(c)
        c += 1
    a, b = [], []
    for j in ("gq0", "gk0", "gq1", "gk1"):
        a += hn(j)
    for t in range(2):
        a += gdn(t)
    for j in ("go0", "go1"):
        a += hn(j)
    side.append(a)
    for _ in range(4):
        mm(c)
        c += 1
    for j in ("fq0", "fq1", "fk0", "fk1"):
        b += hn(j)
    side.append(b)
    mm(c)
    mm(c + 1)
    c += 2
    for h in range(NH):
        b += attend("fox", h)
    for _ in range(6):
        mm(c)
        c += 1
    for h in range(NH):
        b += stick(h)
    if b not in side:
        side.append(b)
    for _ in range(14):
        mm(c, 2)
        c += 1
    while b:
        hook(1)
    for br in (2, 0):
        pl.add("act", "yh", br)
        pl.add("dve", "yl", br)
        for _ in range(2):
            mm(c, 2)
            c += 1
    drain()
    pl.add("act", "yh", 1)
    pl.add("dve", "yl", 1)
    for _ in range(2):
        mm(c)
        c += 1
    for q in range(4):
        pl.add("dve", "mix", q)
        pl.add("act", "mixh", q)
        pl.add("dve", "mixl", q)
    ready["x"] = [("mixl", 3)]
    pl.add("pool", "mem_load")
    for _ in range(4):
        mm(c)
        c += 1
    norm("norm_mem", "m1")
    for _ in range(4):
        mm(c)
        c += 1
    norm("norm_xq")
    for j in ("mk0", "mk1"):
        side.append(hn(j))
    for _ in range(2):
        mm(c)
        c += 1
    drain()
    for j in ("mq0", "mq1"):
        side.append(hn(j))
    drain()
    for lane in range(2):
        side.append(attend("mem", lane) + attend("mem", lane + 2))
    drain()
    mm(c)
    mm(c + 1)
    c += 2
    norm("norm_ffn")
    pl.add("pool", "gain_load", 0)
    for _ in range(KF + KF // 2):
        mm(c)
        c += 1
    norm("ffn1_pre_g_2")
    for _ in range(KF + KF // 2):
        mm(c)
        c += 1
    pl.add("pool", "gain_load", 1)
    norm("mix_pre_g_2")
    pl.add("pool", "mem2_load")
    for _ in range(4):
        mm(c)
        c += 1
    norm("mem_g_2", "m2")
    pl.add("pool", "pool_tables")
    for _ in range(4):
        mm(c)
        c += 1
    for lane in range(2):
        side.append(sum((attend("moba", h) for h in range(lane, 8, 2)), []))
    windows = [[("dve", "pl_win", g)] for g in range(4)]
    for _ in range(8):
        mm(c)
        c += 1
        if windows:
            pl.add(*windows.pop(0)[0])
    drain()
    for g in range(4):
        pl.add("pe", "pl_mm", g)
        pl.add("act", "pl_h", g)
        pl.add("dve", "pl_l", g)
    ready["y5"] = [("ol", "moba", 6), ("ol", "moba", 7), ("pl_l", 3)]
    for _ in range(4):
        mm(c)
        c += 1
    pl.add("pool", "gain_load", 2)
    norm("xa_pre_g_2")
    for _ in range(4):
        mm(c)
        c += 1
    for lane in range(2):
        side.append(attend("xa", lane) + attend("xa", lane + 2))
    drain()
    ready["y5"] = [("ol", "xa", 2), ("ol", "xa", 3)]
    for _ in range(4):
        mm(c)
        c += 1
    pl.add("pool", "gain_load", 3)
    norm("ffn2_pre_g_2")
    for _ in range(KF + KF // 2):
        mm(c)
        c += 1
    assert c == n, (c, n)
    return pl


def two_blocks_kernel(nc, w, out):
    chunks = build_chunks(w)
    plan = build_plan(chunks)
    COL, n_first, n_cols = param_columns()

    with ExitStack() as fixed:
        def sb(name, shape, dt=F32, stack=fixed):
            return stack.enter_context(nc.sbuf_tensor(name, shape, dt))

        raw = [sb(f"raw{i}", [P, 2048]) for i in range(RING)]
        whi = [sb(f"whi{i}", [P, 2048], F32R) for i in range(RING)]
        wlo = [sb(f"wlo{i}", [P, 2048], F32R) for i in range(RING)]
        x = sb("x_tok", [P, NT, D])
        xh = sb("xh", [P, KD, T], F32R)
        xl = sb("xl", [P, KD, T], F32R)
        ident = sb("ident", [P, P])
        ones = sb("ones", [P, P])
        cmask = sb("cmask", [P, NT, T])
        sbm = sb("sbm", [P, P])
        sba = sb("sba", [P, P])
        tri = sb("tri", [P, P])
        gda = sb("gda", [P, P])
        gdat = sb("gdat", [P, P])
        strict = sb("strict", [P, P])
        lev = sb("lev", [P, 6, P])
        sel = sb("sel", [4, NH, T])
        pcol = sb("pcol", [P, 3 * P])
        cf = sb("cf", [4, T])
        ncf = sb("ncf", [4, T])
        gc = sb("gc", [4, T])
        ngc = sb("ngc", [4, T])
        gcols = sb("gcols", [P, NT, 3, 4])
        small = sb("small", [P, 64])
        diag = sb("diag", [P, NT, P])
        eps = small[:, 0:1]
        bst = small[:, 4:28].rearrange("p (t s) -> p t s", t=NT)
        mv = small[:, 28:32].rearrange("p (t s) -> p t s", t=NT)
        ms = small[:, 32:34]
        rn = small[:, 34:36]
        fbias, alog, dtb, ealog = (small[0:4, 36 + i:37 + i] for i in range(4))
        gsc = small[:, 40:41]
        nmx = [small[:, 42:44], small[:, 44:46]]
        rsm = [small[:, 46:48], small[:, 48:50]]
        rrc = [small[:, 50:52], small[:, 52:54]]

        r1 = ExitStack()
        sq_ = sb("sq_", [P, NH, T], stack=r1)
        fq_ = sb("fq_", [P, NH, T], stack=r1)
        gq_ = sb("gq_", [P, NH, T], stack=r1)
        gates = sb("gates", [P, 24, T], stack=r1)
        r1a = ExitStack()
        fk_ = sb("fk_", [P, NH, T], stack=r1a)
        sk_ = sb("sk_", [P, NH, T], stack=r1a)
        fv_ = sb("fv_", [P, NT, 512], stack=r1a)
        sv_ = sb("sv_", [P, NT, 512], stack=r1a)
        S1 = sb("S1", [P, 512], stack=r1a)
        PT1 = sb("PT1", [P, 512], stack=r1a)
        gk_ = sb("gk_", [P, NH, T], stack=r1a)
        gv_ = sb("gv_", [P, NH, T], stack=r1a)
        gz_ = sb("gz_", [P, NH, T], stack=r1a)
        gM, gAT, gX, gY, gU, gMs0, gMs1, gKb, gVb, gKt, gS = (
            sb(nm, [P, NH, P], stack=r1a) for nm in
            ("gM", "gAT", "gX", "gY", "gU", "gMs0", "gMs1", "gKb", "gVb", "gKt", "gS"))
        gMs = [gMs0, gMs1]
        r1a.close()
        r1b = ExitStack()
        ybh, ybl = {}, {}
        for br in (2, 0, 1):
            ybh[br] = sb(f"ybh{br}", [P, NH, T], F32R, stack=r1b)
            ybl[br] = sb(f"ybl{br}", [P, NH, T], F32R, stack=r1b)
        r1b.close()
        r1.close()
        r2 = ExitStack()
        memx = sb("memx", [P, NT, D], stack=r2)
        mh = sb("mh", [P, KD, T], F32R, stack=r2)
        ml = sb("ml", [P, KD, T], F32R, stack=r2)
        mk_ = sb("mk_", [P, NH, T], stack=r2)
        mv_ = sb("mv_", [P, NT, 512], stack=r2)
        mq_ = sb("mq_", [P, NH, T], stack=r2)
        S2 = [sb(f"S2{i}", [P, 512], stack=r2) for i in range(2)]
        PT2 = [sb(f"PT2{i}", [P, 512], stack=r2) for i in range(2)]
        y2h = sb("y2h", [P, NH, T], F32R, stack=r2)
        y2l = sb("y2l", [P, NH, T], F32R, stack=r2)
        r2.close()
        r3 = ExitStack()
        gain = sb("gain", [P, D], stack=r3)
        r3f = ExitStack()
        hh = sb("hh", [P, KF, T], F32R, stack=r3f)
        hl = sb("hl", [P, KF, T], F32R, stack=r3f)
        CA = [sb(f"CA{i}", [P, 2, 512], stack=r3f) for i in range(2)]
        SG = [sb(f"SG{i}", [P, 512], stack=r3f) for i in range(2)]
        ptmp = sb("ptmp", [P, 512], stack=r3f)
        r3f.close()
        r5 = ExitStack()
        mem2 = sb("mem2", [P, NT, D], stack=r5)
        m2h = sb("m2h", [P, KD, T], F32R, stack=r5)
        m2l = sb("m2l", [P, KD, T], F32R, stack=r5)
        xk_ = sb("xk_", [P, KD, T], stack=r5)
        xv_ = sb("xv_", [P, NT, D], stack=r5)
        qk_ = sb("qk_", [P, KD, T], stack=r5)
        bv_ = sb("bv_", [P, NT, 512], stack=r5)
        y5h = sb("y5h", [P, KD, T], F32R, stack=r5)
        y5l = sb("y5l", [P, KD, T], F32R, stack=r5)
        S5 = [sb(f"S5{i}", [P, 512], stack=r5) for i in range(2)]
        PT5 = [sb(f"PT5{i}", [P, 512], stack=r5) for i in range(2)]
        poolw = sb("poolw", [P, 4, P], stack=r5)
        win = sb("win", [P, 2, T], stack=r5)
        r5.close()
        r3.close()
        pin = mem2[:, 0, :].rearrange("p (g t) -> p g t", g=4)
        rcnt = mem2[:, 1, :].rearrange("p (g t) -> p g t", g=4)
        dist = cmask

        banks = fixed.enter_context(nc.psum_tensor("banks", [P, 8, 512], F32))

        def bank(i):
            return banks[:, i, :]

        def sem(name):
            return fixed.enter_context(nc.semaphore(name))

        pe_done, act_done, dve_done, pool_done = (sem(s) for s in ("pe_done", "act_done", "dve_done", "pool_done"))
        DONE = {"pe": pe_done, "act": act_done, "dve": dve_done, "pool": pool_done}
        raw_in = [sem(f"raw_in{i}") for i in range(RING)]
        x_in, par_in, mem_in, mem2_in, gains_in, pw_in, out_done = (
            sem(s) for s in ("x_in", "par_in", "mem_in", "mem2_in", "gains_in", "pw_in", "out_done"))
        act_link, dve_link, pool_link = sem("act_link"), sem("dve_link"), sem("pool_link")

        def at(name, *args):
            return plan.number[(name, *args)]

        landed, used = [], [0] * RING
        for c, ch in enumerate(chunks):
            used[c % RING] += 16 * len(ch["srcs"])
            landed.append(used[c % RING])

        N_PAR = 15 + 5 + 3
        POSTS = [c for c, ch in enumerate(chunks) if ch["evac"] == "post"]

        def width(ch):
            return {"A": 256, "S": 256, "V": 512, "O": 512, "R": 1024}[ch["kind"]]

        def chunk_of(to, i):
            return max(c for c, ch in enumerate(chunks)
                       if (ch.get("to") == to or ch["evac"] == to) and (i is None or ch.get("i") == i))

        def pair(f, i):
            cg, cu = (c for c, ch in enumerate(chunks) if ch.get("f") == f and ch.get("i") == i)
            return cg, cu

        def pin_tmp(c):
            a, b = SG if chunks[c]["name"].startswith("ffn") else S5
            return [a[:, :], b[:, :]]

        def run(e, engine, steps):
            n = 0
            for eng, name, args in plan.steps:
                if eng != engine:
                    continue
                if n and engine != "pe" and name not in ("hi", "lo"):
                    e.wait_ge(DONE[engine], n)
                steps[name](*args)
                n += 1

        def gate_row(i):
            return gates[0:4, i, :]

        W2, E2, GBR, EBR = gates[0:4, 0:2, :], gates[0:4, 2:4, :], gate_row(4), gate_row(5)
        SP2, BETA, GLOG, TAIL, ETAIL, EGC, BEGC = gates[0:4, 6:8, :], *(gate_row(i) for i in range(8, 14))
        prow = gates[:, 14:17, 0:P]
        lev_tmp = [gates[:, 17 + i, 0:P] for i in range(2)]

        XHL = {"x": (xh, xl), "m1": (mh, ml), "m2": (m2h, m2l), "ym": (y2h, y2l), "y5": (y5h, y5l),
               "h0": (hh, hl), "h1": (hh, hl), "h2": (hh, hl)}
        for br in range(3):
            XHL[f"y{br}"] = (ybh[br], ybl[br])
        NORM = {"norm_mix": (x, xh, xl), "norm_xq": (x, xh, xl), "norm_ffn": (x, xh, xl), "norm_mem": (memx, mh, ml),
                "ffn1_pre_g_2": (x, xh, xl), "mix_pre_g_2": (x, xh, xl), "xa_pre_g_2": (x, xh, xl),
                "ffn2_pre_g_2": (x, xh, xl), "mem_g_2": (mem2, m2h, m2l)}
        TO = {"fq": fq_, "fk": fk_, "sq": sq_, "sk": sk_, "mk": mk_, "mq": mq_, "qk": qk_, "xk": xk_, "xq": qk_,
              "pin": pin, "fv": fv_, "sv": sv_, "mv": mv_, "bv": bv_, "xv0": xv_[:, :, 0:512], "xv1": xv_[:, :, 512:1024]}

        def pcolumn(name, i=0):
            return pcol[:, COL[name] + i:COL[name] + i + 1]

        HN = {}
        for i in range(2):
            s = slice(2 * i, 2 * i + 2)
            HN[f"gq{i}"] = (gq_[:, s, :], gKb, gVb, 4, None, 1.0, float(HD) ** -0.5, None)
            HN[f"gk{i}"] = (gk_[:, s, :], gKb, gVb, 4, None, 1.0, 1.0, None)
            HN[f"go{i}"] = (gq_[:, s, :], gKb, gVb, 4, pcolumn("gdn_onorm"), 1.0 / HD, 1.0, gz_[:, s, :])
            HN[f"fq{i}"] = (fq_[:, s, :], S1, PT1, 6, gsc, 1.0 / HD, 1.0, None)
            HN[f"fk{i}"] = (fk_[:, s, :], S1, PT1, 6, pcolumn("fox_knorm"), 1.0 / HD, 1.0, None)
            HN[f"mq{i}"] = (mq_[:, s, :], S2[0], PT2[0], 4, pcolumn("mq_norm"), 1.0 / HD, 1.0, None)
            HN[f"mk{i}"] = (mk_[:, s, :], S2[0], PT2[0], 4, pcolumn("mk_norm"), 1.0 / HD, 1.0, None)

        HN_BEFORE = {}
        for jobs in (("gq0", "gk0", "gq1", "gk1", "go0", "go1"), ("fq0", "fq1", "fk0", "fk1"), ("mk0", "mk1", "mq0", "mq1")):
            HN_BEFORE |= dict(zip(jobs[1:], jobs))

        FACTOR = {"fox": 1.0, "mem": float(HD) ** -0.5, "moba": 64.0 ** -0.5, "xa": 256.0 ** -0.5}
        SLOPE = [2.0 ** (-(h + 1)) for h in range(8)]

        def lane(kind, h):
            l = 1 if kind == "fox" else h % 2
            s, pt = {"fox": (S1, PT1), "mem": (S2[l], PT2[l])}.get(kind, (S5[l], PT5[l]))
            return s, pt, 4 + 2 * l, 5 + 2 * l, nmx[l], rsm[l], rrc[l]

        def before(kind, h):
            d = 1 if kind == "fox" else 2
            return h - d if h >= d else None

        def values(kind, h):
            return {"fox": lambda: fv_[:, :, h * HD:(h + 1) * HD], "mem": lambda: mv_[:, :, h * HD:(h + 1) * HD],
                    "moba": lambda: bv_[:, :, h * 64:(h + 1) * 64], "xa": lambda: xv_[:, :, h * 256:(h + 1) * 256]}[kind]()

        def mat(t):
            return t[:, :].rearrange("p (a b) -> p a b", a=2) if len(t.shape) == 2 else t.rearrange("p h t -> p (h t)").rearrange("p (a b) -> p a b", a=2)

        def per_head(t):
            return t.rearrange("p (h e) -> p h e", h=NH)

        def flat(t):
            return t.rearrange("p a b -> p (a b)") if len(t.shape) == 3 else t

        block = fixed.enter_context(nc.Block())

        @block.sync
        def _(sp):
            sp.dma_start(x[:, :, :], w["x"].rearrange("(t p) d -> p t d", p=P)).then_inc(x_in, 16)
            for c, ch in enumerate(chunks):
                if c >= RING:
                    sp.wait_ge(dve_done, at("lo", c - RING))
                for (a, b), src in ch["srcs"]:
                    dst = raw[c % RING][:, 0:src.shape[1] * width(ch)].rearrange("p (k n) -> p k n", n=width(ch))
                    sp.dma_start(dst[:, :, a:b], src).then_inc(raw_in[c % RING], 16)
            sp.wait_ge(dve_done, at("post2", len(chunks) - 1))
            sp.dma_start(out.rearrange("(t p) d -> p t d", p=P), x[:, :, :]).then_inc(out_done, 16)
            sp.wait_ge(out_done, 16)

        @block.gpsimd
        def _(pool):
            linked = [0]

            def link(ins):
                linked[0] += 1
                ins.then_inc(pool_link, 1)
                pool.wait_ge(pool_link, linked[0])

            def select(outp, inp, pattern, base, cm, fill, op=ALU.is_ge):
                return pool.affine_select(out=outp, in_=inp, pattern=pattern, compare_op=op, fill=fill,
                                          base=base, channel_multiplier=cm)

            def consts():
                link(pool.memset(ident[:, :], 0.0))
                link(select(ident[:, :], ident[:, :], [[-1, P]], 0, 1, 1.0, ALU.not_equal))
                link(pool.memset(ones[:, :], 1.0))
                pool.memset(eps, EPS).then_inc(pool_done, 1)

            def consts2():
                link(pool.memset(sel[:, :, :], 0.0))
                link(select(sel[:, :, :], sel[:, :, :], [[-1, NH], [0, T]], 0, 1, 1.0, ALU.not_equal))
                link(pool.memset(cmask[:, :, :], 0.0))
                link(select(cmask[:, :, :], cmask[:, :, :], [[P, NT], [-1, T]], 0, 1, NEG))
                link(select(sbm[:, :], ones[:, :], [[1, P]], -1, -1, 0.0))
                link(pool.memset(sba[:, :], 0.0))
                link(select(sba[:, :], sba[:, :], [[1, P]], -1, -1, NEG))
                link(select(tri[:, :], ones[:, :], [[-1, P]], 0, 1, 0.0))
                link(pool.memset(gda[:, :], 0.0))
                link(select(gda[:, :], gda[:, :], [[-1, P]], 0, 1, NEG))
                link(select(gda[:, :], gda[:, :], [[CH, 2], [0, CH]], CH - 1, -1, NEG))
                link(pool.memset(gdat[:, :], 0.0))
                link(select(gdat[:, :], gdat[:, :], [[1, P]], 0, -1, NEG))
                link(select(gdat[:, :], gdat[:, :], [[-CH, 2], [0, CH]], 0, 1, NEG))
                link(select(strict[:, :], ones[:, :], [[-1, P]], -1, 1, 0.0))
                small_block = ident[:, :]
                for l in range(6):
                    s = 2 << l
                    big = lev_tmp[l % 2]
                    link(select(big, ones[:, :], [[-s, P // s], [0, s]], 0, 1, 0.0))
                    link(select(big, big, [[s, P // s], [0, s]], s - 1, -1, 0.0))
                    ins = pool.tensor_tensor(lev[:, l, :], big, small_block, ALU.subtract)
                    if l < 5:
                        link(ins)
                    small_block = big
                ins.then_inc(pool_done, 1)

            def g_eye(t):
                if t:
                    pool.wait_ge(dve_done, at("r_s", 0, 1))
                    pool.wait_ge(pe_done, at("g_uw", 0))
                eye = ident[:, :].unsqueeze(1).to_broadcast([P, NH, P])
                pool.tensor_copy(gX[:, :, :], eye)
                pool.tensor_copy(gY[:, :, :], eye).then_inc(pool_done, 1)

            def l_mask(t, l):
                pool.wait_ge(dve_done, at("g_m", t))
                if l >= 2:
                    pool.wait_ge(pe_done, at("l_u", t, l - 2))
                elif t:
                    pool.wait_ge(dve_done, at("r_s", 0, 1))
                pool.tensor_tensor(gMs[l % 2][:, :, :], gM[:, :, :], lev[:, l, :].unsqueeze(1).to_broadcast([P, NH, P]),
                                   ALU.mult).then_inc(pool_done, 1)

            def mem_load():
                pool.wait_ge(dve_done, at("mixl", 3))
                pool.dma_start(memx[:, :, :], w["mem"].rearrange("(t p) d -> p t d", p=P)).then_inc(mem_in, 16)
                pool.memset(small[:, 60:61], 0.0).then_inc(pool_done, 1)

            def gain_load(i):
                if i:
                    pool.wait_ge(dve_done, at("post2", POSTS[i - 1]))
                else:
                    pool.wait_ge(dve_done, at("nl", "norm_ffn", 3))
                name = ("ffn1_post_g_2", "mix_post_g_2", "xa_post_g_2", "ffn2_post_g_2")[i]
                pool.dma_start(gain[:, :], w[name].to_broadcast([P, D])).then_inc(gains_in, 16)
                pool.memset(small[:, 61:62], 0.0).then_inc(pool_done, 1)

            def mem2_load():
                pool.wait_ge(dve_done, at("nl", "mix_pre_g_2", 3))
                pool.dma_start(mem2[:, :, :], w["mem_2"].rearrange("(t p) d -> p t d", p=P)).then_inc(mem2_in, 16)
                pool.dma_start(poolw[:, :, :], w["pool_w_2"].rearrange("(g c) d -> c g d", c=P)).then_inc(pw_in, 16)
                pool.memset(small[:, 62:63], 0.0).then_inc(pool_done, 1)

            def pool_tables():
                pool.wait_ge(dve_done, at("nl", "mem_g_2", 3))
                link(pool.iota(dist[:, :, :], [[P, NT], [-1, T]], 0, 1, allow_small_or_imprecise_dtypes=True))
                link(select(dist[:, :, :], dist[:, :, :], [[P, NT], [-1, T]], 0, 1, -NEG))
                link(pool.iota(rcnt[:, :, :], [[0, 4], [1, T]], 1, 0, allow_small_or_imprecise_dtypes=True))
                for g in range(4):
                    ins = pool.tensor_scalar(rcnt[:, g, :], rcnt[:, g, :], float(2 << g), None, ALU.min)
                ins.then_inc(pool_done, 1)

            run(pool, "pool", locals())

        @block.tensor
        def _(pe):
            def params():
                pe.wait_ge(par_in, 16 * N_PAR)
                pe.wait_ge(pool_done, at("consts"))
                for j, n in enumerate((n_first, P, n_cols - 2 * P)):
                    ins = pe.matmul(bank(4)[:, j * P:j * P + n], prow[0:n, j, :], ident[0:n, 0:n], start=True, stop=True)
                ins.then_inc(pe_done, 1)

            def mm(c, part):
                ch = chunks[c]
                slot, (Xh, Xl), b = c % RING, XHL[ch["x"]], ch["banks"]
                if part == 0:
                    pe.wait_ge(dve_done, at("lo", c))
                    for step in plan.ready[c]:
                        pe.wait_ge(DONE[plan.engine[step[0]]], at(*step))
                    for step in plan.bank_wait.get(("mm", c, 0), []):
                        pe.wait_ge(DONE[plan.engine[step[0]]], at(*step))
                n = width(ch)
                wh, wl = (t[slot][:, :].rearrange("p (k n) -> p k n", n=n) for t in (whi, wlo))
                if ch["kind"] == "S":
                    for col, o in ([(0, bank(0)[:, 0:T]), (P, bank(0)[:, T:2 * T])] if part == 0 else [(P + 4, bank(1)[0:124, 0:T])]):
                        m = min(P, 256 - col)
                        for k in range(KD):
                            for i, (a, v) in enumerate(((wh, Xh), (wh, Xl), (wl, Xh))):
                                ins = pe.matmul(o[0:m, :], a[:, k, col:col + m], v[:, k, :],
                                                start=(k == 0 and i == 0), stop=(k == KD - 1 and i == 2))
                elif ch["kind"] == "A":
                    for k in range(KD):
                        for i, (a, v) in enumerate(((wh, Xh), (wh, Xl), (wl, Xh))):
                            ins = pe.matmul(bank(b[0])[:, part * T:(part + 1) * T], a[:, k, part * P:(part + 1) * P], v[:, k, :],
                                            start=(k == 0 and i == 0), stop=(k == KD - 1 and i == 2))
                elif ch["kind"] == "O":
                    for m in range(2):
                        o = (2 * part + m) * P
                        for k in range(NH):
                            for i, (a, v) in enumerate(((wh, Xh), (wh, Xl), (wl, Xh))):
                                ins = pe.matmul(bank(b[part])[:, m * T:(m + 1) * T], a[:, k, o:o + P], v[:, k, :],
                                                start=(k == 0 and i == 0), stop=(k == NH - 1 and i == 2))
                elif ch["kind"] == "V":
                    for kk in range(2 * part, 2 * part + 2):
                        k = 4 * ch["half"] + kk
                        for t in range(NT):
                            for i, (v, a) in enumerate(((Xh, wh), (Xh, wl), (Xl, wh))):
                                ins = pe.matmul(bank(b[t]), v[:, k, t * P:(t + 1) * P], a[:, kk, :],
                                                start=(k == 0 and i == 0), stop=(k == KD - 1 and i == 2))
                else:
                    k = 2 * ch["j"] + part
                    for t in range(NT):
                        for nb in range(2):
                            for i, (v, a) in enumerate(((Xh, wh), (Xh, wl), (Xl, wh))):
                                ins = pe.matmul(bank(b[2 * t + nb]), v[:, k, t * P:(t + 1) * P], a[:, part, nb * 512:(nb + 1) * 512],
                                                start=(k == 0 and i == 0), stop=(ch["last"] and part == 1 and i == 2))
                ins.then_inc(pe_done, 1)

            def nt(name, j):
                src = NORM[name][0]
                pe.wait_ge(dve_done, at("nd", name))
                for step in plan.bank_wait[("nt", name, j)]:
                    pe.wait_ge(DONE[plan.engine[step[0]]], at(*step))
                for k in range(2):
                    for t in range(NT):
                        kt = 2 * j + k
                        ins = pe.matmul(bank(j)[:, k * T + t * P:k * T + (t + 1) * P], src[:, t, kt * P:(kt + 1) * P],
                                        diag[:, t, :], start=True, stop=True)
                ins.then_inc(pe_done, 1)

            def rows6():
                pe.wait_ge(dve_done, at("rows5"))
                pe.wait_ge(dve_done, at("params_c"))
                for t in range(NT):
                    for j, row in enumerate((BETA, BEGC, ETAIL)):
                        o = (t * 3 + j) * 4
                        ins = pe.matmul(bank(4)[:, o:o + 4], row[:, t * P:(t + 1) * P], ident[0:4, 0:4], start=True, stop=True)
                ins.then_inc(pe_done, 1)

            def hn_sum(job):
                dst, sq, rr, b, *_ = HN[job]
                pe.wait_ge(act_done, at("hn_sq", job))
                if job == "gq0":
                    pe.wait_ge(dve_done, at("rows7"))
                if job == "go0":
                    pe.wait_ge(dve_done, at("r_s", 1, 1))
                elif job in HN_BEFORE:
                    pe.wait_ge(dve_done, at("hn_mul", HN_BEFORE[job]))
                pe.matmul(bank(b), ones[:, :], flat(sq[:]), start=True, stop=True).then_inc(pe_done, 1)

            def g_dec(t):
                pe.wait_ge(dve_done, at("hn_mul", "gk1"))
                pe.wait_ge(pool_done, at("consts2"))
                if t:
                    pe.wait_ge(act_done, at("r_oc", 0, 1))
                    pe.wait_ge(dve_done, at("r_s", 0, 1))
                s = slice(t * P, (t + 1) * P)
                for h in range(NH):
                    e = slice(h * P, (h + 1) * P)
                    pe.matmul(bank(4)[:, e], gc[0:4, s], sel[0:4, h, 0:P], start=True, stop=False)
                    pe.matmul(bank(4)[:, e], sel[0:4, h, 0:P], ngc[0:4, s], start=False, stop=True)
                for h in range(NH):
                    e = slice(h * P, (h + 1) * P)
                    pe.matmul(bank(5)[:, e], sel[0:4, h, 0:P], gc[0:4, s], start=True, stop=False)
                    ins = pe.matmul(bank(5)[:, e], ngc[0:4, s], sel[0:4, h, 0:P], start=False, stop=True)
                ins.then_inc(pe_done, 1)

            def g_kk(t):
                pe.wait_ge(dve_done, at("g_mask", t))
                s = slice(t * P, (t + 1) * P)
                for h in range(NH):
                    pe.matmul(bank(4)[:, h * P:(h + 1) * P], gk_[:, h, s], gk_[:, h, s], start=True, stop=True)
                for h in range(NH):
                    ins = pe.matmul(bank(5)[:, h * P:(h + 1) * P], gk_[:, h, s], gq_[:, h, s], start=True, stop=True)
                ins.then_inc(pe_done, 1)

            def g_turn(t):
                pe.wait_ge(dve_done, at("g_m", t))
                s = slice(t * P, (t + 1) * P)
                for b, src in ((4, gk_), (5, gv_)):
                    for h in range(NH):
                        ins = pe.matmul(bank(b)[:, h * P:(h + 1) * P], src[:, h, s], ident[:, :], start=True, stop=True)
                ins.then_inc(pe_done, 1)

            def l_u(t, l):
                pe.wait_ge(pool_done, at("l_mask", t, l))
                if l:
                    pe.wait_ge(dve_done, at("l_upd", t, l - 1))
                else:
                    pe.wait_ge(act_done, at("g_kb", t))
                    pe.wait_ge(dve_done, at("g_vb", t))
                for h in range(NH):
                    ins = pe.matmul(bank(4)[:, h * P:(h + 1) * P], gMs[l % 2][:, h, :], gY[:, h, :], start=True, stop=True)
                ins.then_inc(pe_done, 1)

            def l_x(t, l):
                pe.wait_ge(act_done, at("l_uc", t, l))
                if l < 5:
                    for h in range(NH):
                        pe.matmul(bank(5)[:, h * P:(h + 1) * P], gU[:, h, :], gX[:, h, :], start=True, stop=True)
                for h in range(NH):
                    ins = pe.matmul(bank(4)[:, h * P:(h + 1) * P], gX[:, h, :], gU[:, h, :], start=True, stop=True)
                ins.then_inc(pe_done, 1)

            def g_uw(t):
                pe.wait_ge(dve_done, at("l_upd", t, 5))
                for h in range(NH):
                    pe.matmul(bank(4)[:, h * P:(h + 1) * P], gY[:, h, :], gVb[:, h, :], start=True, stop=True)
                for h in range(NH):
                    ins = pe.matmul(bank(5)[:, h * P:(h + 1) * P], gKb[:, h, :], gY[:, h, :], start=True, stop=True)
                ins.then_inc(pe_done, 1)

            def g_bc(t):
                pe.wait_ge(dve_done, at("g_u", t))
                for h in range(NH):
                    ins = pe.matmul(bank(4)[:, h * P:(h + 1) * P], sel[0:4, h, 0:P], gc[0:4, t * P:(t + 1) * P], start=True, stop=True)
                ins.then_inc(pe_done, 1)

            def r_ws(t, j):
                r = slice(j * CH, (j + 1) * CH)
                pe.wait_ge(act_done, at("g_w", t))
                pe.wait_ge(dve_done, at("g_qg", t))
                if j:
                    pe.wait_ge(dve_done, at("r_s", t, 0))
                for h in range(NH):
                    ins = pe.matmul(bank(4)[r, h * P:(h + 1) * P], gU[:, h, r], gS[:, h, :], start=True, stop=True)
                ins.then_inc(pe_done, 1)

            def r_o(t, j):
                r = slice(j * CH, (j + 1) * CH)
                s = slice(t * P + j * CH, t * P + (j + 1) * CH)
                pe.wait_ge(dve_done, at("r_vn", t, j))
                if j:
                    pe.wait_ge(act_done, at("r_oc", t, 0))
                for h in range(NH):
                    o = bank(5)[:, h * CH:(h + 1) * CH]
                    pe.matmul(o, gS[:, h, :], gq_[:, h, s], start=True, stop=False)
                    pe.matmul(o, gMs0[r, h, :], gAT[r, h, r], start=False, stop=True)
                for h in range(NH):
                    ins = pe.matmul(bank(4)[:, h * P:(h + 1) * P], gKt[r, h, :], gMs0[r, h, :], start=True, stop=True)
                ins.then_inc(pe_done, 1)

            def sc(kind, h):
                s_, pt_, b, *_ = lane(kind, h)
                p = before(kind, h)
                if p is not None:
                    pe.wait_ge(act_done, at("oc", kind, p))
                    if kind != "fox":
                        pe.wait_ge(dve_done, at("ol", kind, p))
                if kind == "fox":
                    pe.wait_ge(dve_done, at("hn_mul", "fk1"))
                    pe.wait_ge(pool_done, at("consts2"))
                elif kind == "mem":
                    pe.wait_ge(dve_done, at("hn_mul", "mq1"))
                elif kind == "moba":
                    pe.wait_ge(act_done, at("copy", chunk_of("qk", 3)))
                else:
                    pe.wait_ge(act_done, at("copy", chunk_of("xq", 3)))
                for t in range(NT):
                    q = slice(t * P, (t + 1) * P)
                    o = bank(b)[:, t * T:(t + 1) * T]
                    if kind == "fox":
                        pe.matmul(o, fq_[:, h, q], fk_[:, h, :], start=True, stop=False)
                        pe.matmul(o, cf[0:4, q], sel[0:4, h, :], start=False, stop=False)
                        ins = pe.matmul(o, sel[0:4, h, 0:P], ncf[0:4, :], start=False, stop=True)
                    elif kind == "mem":
                        ins = pe.matmul(o, mq_[:, h, q], mk_[:, h, :], start=True, stop=True)
                    elif kind == "moba":
                        r = slice(64 * (h % 2), 64 * (h % 2) + 64)
                        ins = pe.matmul(o, qk_[r, h // 2, q], qk_[r, 4 + h // 2, :], start=True, stop=True)
                    else:
                        for k in range(2):
                            ins = pe.matmul(o, qk_[:, 2 * h + k, q], xk_[:, 2 * h + k, :], start=(k == 0), stop=(k == 1))
                ins.then_inc(pe_done, 1)

            def pt(kind, h):
                s_, pt_, b0, b, *_ = lane(kind, h)
                pe.wait_ge(dve_done, at("pn", kind, h))
                p = before(kind, h)
                if p is not None:
                    pe.wait_ge(act_done, at("pc", kind, p))
                for kb in range(2):
                    for t in range(NT):
                        ins = pe.transpose(bank(b)[:, kb * T + t * P:kb * T + (t + 1) * P],
                                           s_[:, t * T + kb * P:t * T + (kb + 1) * P], ident[:, :])
                ins.then_inc(pe_done, 1)

            def pv(kind, h):
                s_, pt_, b, *_ = lane(kind, h)
                pe.wait_ge(act_done, at("pc", kind, h))
                if kind in ("mem", "xa", "moba", "fox"):
                    pe.wait_ge(act_done, at("copy", chunk_of({"mem": "mv", "xa": "xv1", "moba": "bv", "fox": "fv"}[kind], None)))
                v = values(kind, h)
                r0 = 64 * (h % 2) if kind == "moba" else 0
                for m in range(2 if kind == "xa" else 1):
                    width_ = 64 if kind == "moba" else P
                    o = bank(b)[r0:r0 + width_, m * T:(m + 1) * T]
                    for kb in range(2):
                        ins = pe.matmul(o, v[:, kb, m * P:m * P + width_], pt_[:, kb * T:(kb + 1) * T], start=(kb == 0), stop=(kb == 1))
                ins.then_inc(pe_done, 1)

            def z_s(h):
                if h:
                    pe.wait_ge(act_done, at("z_oc", h - 1))
                else:
                    pe.wait_ge(act_done, at("oc", "fox", NH - 1))
                    pe.wait_ge(act_done, at("copy", chunk_of("sk", 1)))
                pe.matmul(bank(6)[:, 0:T], sk_[:, h, 0:P], sq_[:, h, :], start=True, stop=True)
                pe.matmul(bank(6)[:, T:T + P], sk_[:, h, P:T], sq_[:, h, P:T], start=True, stop=True).then_inc(pe_done, 1)

            def z_rc(h):
                pe.wait_ge(dve_done, at("z_lk", h))
                if h:
                    pe.wait_ge(dve_done, at("z_w", h - 1))
                pe.matmul(bank(7)[:, T:T + P], tri[:, :], PT1[:, T:T + P], start=True, stop=True)
                pe.matmul(bank(7)[:, 0:T], tri[:, :], PT1[:, 0:T], start=True, stop=False)
                pe.matmul(bank(7)[:, P:T], ones[:, :], PT1[:, T:T + P], start=False, stop=True).then_inc(pe_done, 1)

            def z_o(h):
                pe.wait_ge(act_done, at("z_x", h))
                pe.wait_ge(act_done, at("copy", chunk_of("sv", None)))
                pe.matmul(bank(6)[:, 0:T], sv_[:, 0, h * HD:(h + 1) * HD], S1[:, 0:T], start=True, stop=False)
                pe.matmul(bank(6)[:, P:T], sv_[:, 1, h * HD:(h + 1) * HD], S1[:, T:T + P], start=False, stop=True).then_inc(pe_done, 1)

            def pl_mm(g):
                pe.wait_ge(dve_done, at("pl_win", g))
                if g == 0:
                    pe.wait_ge(pw_in, 16)
                    pe.wait_ge(dve_done, at("ol", "moba", 6))
                    pe.wait_ge(dve_done, at("ol", "moba", 7))
                pe.matmul(bank(4 + g)[:, 0:T], poolw[:, g, :], pin[:, g, :], start=True, stop=True).then_inc(pe_done, 1)

            run(pe, "pe", locals())

        @block.scalar
        def _(act):
            linked = [0]

            def link(ins):
                linked[0] += 1
                ins.then_inc(act_link, 1)
                act.wait_ge(act_link, linked[0])

            prm = [("norm_mix", 8), ("norm_xq", 8), ("norm_mem", 8), ("norm_ffn", 8), ("ffn1_pre_g_2", 8), ("mix_pre_g_2", 8),
                   ("xa_pre_g_2", 8), ("mem_g_2", 8), ("ffn2_pre_g_2", 8), ("gdn_conv", 48), ("fox_qnorm", 1),
                   ("fox_knorm", 1), ("gdn_onorm", 1), ("mq_norm", 1), ("mk_norm", 1)]
            for name, n in prm:
                r = COL[name]
                act.dma_start(prow[r:r + n, 0, :], w[name].rearrange("a (r c) -> (a r) c", c=P)).then_inc(par_in, 16)
            for name, n in (("ffn_conv", 6 * KF), ("ffn_conv_b", 2 * KF), ("gate_bias", 24), ("pool_scale_2", 4)):
                src, r = w[name].rearrange("a (r c) -> (a r) c", c=P), COL[name]
                done = 0
                while done < n:
                    j, p0 = divmod(r + done, P)
                    k = min(n - done, P - p0)
                    act.dma_start(prow[p0:p0 + k, j, :], src[done:done + k, :]).then_inc(par_in, 16)
                    done += k
            for name, dst in (("fox_fbias", fbias), ("gdn_a_log", alog), ("gdn_dt_bias", dtb)):
                act.dma_start(dst, w[name].rearrange("a h -> h a")).then_inc(par_in, 16)

            def hi(c):
                act.wait_ge(raw_in[c % RING], landed[c])
                if c >= RING:
                    act.wait_ge(pe_done, at("mm", c - RING, 1))
                act.activation(whi[c % RING][:, :], raw[c % RING][:, :], ACT.Copy).then_inc(act_done, 1)

            def nr(name):
                act.wait_ge(dve_done, at("ns", name))
                act.wait_ge(pool_done, at("consts"))
                link(act.activation(rn, ms, ACT.Ln, bias=eps))
                act.activation(rn, rn, ACT.Exp, scale=-0.5).then_inc(act_done, 1)

            def nh(name, j):
                act.wait_ge(pe_done, at("nt", name, j))
                act.wait_ge(dve_done, at("params_c"))
                gname = name
                for k in range(2):
                    kt = 2 * j + k
                    ins = act.activation(NORM[name][1][:, kt, :], bank(j)[:, k * T:(k + 1) * T], ACT.Copy, scale=pcolumn(gname, kt))
                ins.then_inc(act_done, 1)

            def rows2():
                act.wait_ge(dve_done, at("rows1"))
                act.activation(ealog, alog, ACT.Exp)
                act.activation(EBR, GBR, ACT.Exp, scale=-1.0)
                link(act.activation(E2, W2, ACT.Abs))
                link(act.activation(E2, E2, ACT.Exp, scale=-1.0))
                act.activation(E2, E2, ACT.Ln, bias=1.0).then_inc(act_done, 1)

            def rows4():
                act.wait_ge(dve_done, at("rows3"))
                act.activation(EGC, gc[:, :], ACT.Exp)
                act.activation(ETAIL, TAIL, ACT.Exp).then_inc(act_done, 1)

            def cv_mul(c):
                i = chunks[c]["i"]
                act.wait_ge(pe_done, at("mm", c, 1))
                dst = (gq_, gk_, gv_)[i // 2]
                for m in range(2):
                    ins = act.activation(dst[:, 2 * (i % 2) + m, :], bank(chunks[c]["banks"][0])[:, m * T:(m + 1) * T], ACT.Copy,
                                         scale=pcolumn("gdn_conv", 3 * 12 + 2 * i + m))
                ins.then_inc(act_done, 1)

            def cv_silu(c):
                i = chunks[c]["i"]
                act.wait_ge(dve_done, at("cv_add", c))
                d = (gq_, gk_, gv_)[i // 2][:, 2 * (i % 2):2 * (i % 2) + 2, :]
                act.activation(d, d, ACT.Silu).then_inc(act_done, 1)

            def copy(c):
                ch = chunks[c]
                act.wait_ge(pe_done, at("mm", c, 1))
                if ch["kind"] == "V":
                    for t in range(NT):
                        ins = act.activation(TO[ch["to"]][:, t, :], bank(ch["banks"][t]), ACT.Copy)
                elif ch["evac"] == "copy":
                    if ch["to"] == "xq" or ch["to"] == "pin":
                        act.wait_ge(dve_done, at("nl", "mem_g_2", 3))
                    ins = act.activation(TO[ch["to"]][:, 2 * ch["i"]:2 * ch["i"] + 2, :],
                                         bank(ch["banks"][0]).rearrange("p (a b) -> p a b", a=2), ACT.Copy)
                elif ch["evac"] == "gz":
                    ins = act.activation(gz_[:, 2 * ch["i"]:2 * ch["i"] + 2, :],
                                         bank(ch["banks"][0]).rearrange("p (a b) -> p a b", a=2), ACT.Silu)
                else:
                    if ch["i"] == 0:
                        act.wait_ge(dve_done, at("rows7"))
                        act.wait_ge(pool_done, at("consts2"))
                    for m in range(2):
                        f = 2 * ch["i"] + m
                        ins = act.activation(gates[:, f, :], bank(ch["banks"][0])[:, m * T:(m + 1) * T], ACT.Sigmoid,
                                             bias=pcolumn("gate_bias", f))
                ins.then_inc(act_done, 1)

            def hn_sq(job):
                dst, sq, rr, b, *_ = HN[job]
                if job in ("mq0", "mk0"):
                    pass
                act.activation(mat(sq), dst, ACT.Square).then_inc(act_done, 1)

            def hn_r(job):
                dst, sq, rr, b, g, inv, f, gate = HN[job]
                act.wait_ge(pe_done, at("hn_sum", job))
                if job in HN_BEFORE:
                    act.wait_ge(dve_done, at("hn_mul", HN_BEFORE[job]))
                link(act.activation(flat(rr[:]), bank(b), ACT.Ln, bias=eps, scale=inv))
                act.activation(flat(rr[:]), flat(rr[:]), ACT.Exp, scale=-0.5).then_inc(act_done, 1)

            def g_exp(t):
                act.wait_ge(dve_done, at("g_mask", t))
                act.activation(gM[:, :, :], gM[:, :, :], ACT.Exp)
                act.activation(gAT[:, :, :], gAT[:, :, :], ACT.Exp).then_inc(act_done, 1)

            def g_kb(t):
                act.wait_ge(pe_done, at("g_turn", t))
                act.wait_ge(dve_done, at("rows7"))
                for h in range(NH):
                    act.activation(gKb[:, h, :], bank(4)[:, h * P:(h + 1) * P], ACT.Copy, scale=gcols[:, t, 1, h:h + 1])
                    ins = act.activation(gKt[:, h, :], bank(4)[:, h * P:(h + 1) * P], ACT.Copy, scale=gcols[:, t, 2, h:h + 1])
                ins.then_inc(act_done, 1)

            def l_uc(t, l):
                act.wait_ge(pe_done, at("l_u", t, l))
                act.activation(gU[:, :, :], per_head(bank(4)), ACT.Copy).then_inc(act_done, 1)

            def g_w(t):
                act.wait_ge(pe_done, at("g_uw", t))
                act.activation(gU[:, :, :], per_head(bank(5)), ACT.Copy).then_inc(act_done, 1)

            def g_egc(t):
                act.wait_ge(pe_done, at("g_bc", t))
                act.activation(gX[:, :, :], per_head(bank(4)), ACT.Exp).then_inc(act_done, 1)

            def r_oc(t, j):
                act.wait_ge(pe_done, at("r_o", t, j))
                s = slice(t * P + j * CH, t * P + (j + 1) * CH)
                act.activation(gq_[:, :, s], bank(5)[:, 0:NH * CH].rearrange("p (h e) -> p h e", h=NH), ACT.Copy).then_inc(act_done, 1)

            def ex(kind, h):
                s_, pt_, b, b2, nm, rs, rc = lane(kind, h)
                act.wait_ge(dve_done, at("sm", kind, h))
                f = FACTOR[kind]
                if before(kind, h) is not None:
                    act.wait_ge(pe_done, at("pt", kind, before(kind, h)))
                src = s_ if kind in ("fox", "moba") else bank(b)
                for t in range(NT):
                    ins = act.activation(s_[:, t * T:(t + 1) * T], src[:, t * T:(t + 1) * T], ACT.Exp, bias=nm[:, t:t + 1],
                                         scale=f, accum_out=rs[:, t:t + 1])
                ins.then_inc(act_done, 1)

            def pc(kind, h):
                s_, pt_, b0, b, *_ = lane(kind, h)
                act.wait_ge(pe_done, at("pt", kind, h))
                if before(kind, h) is not None:
                    act.wait_ge(pe_done, at("pv", kind, before(kind, h)))
                act.activation(pt_[:, :], bank(b), ACT.Copy).then_inc(act_done, 1)

            def oc(kind, h):
                s_, pt_, b, *_ = lane(kind, h)
                act.wait_ge(pe_done, at("pv", kind, h))
                if kind == "fox":
                    ins = act.activation(fq_[:, h, :], bank(b)[:, 0:T], ACT.Copy)
                elif kind == "mem":
                    ins = act.activation(y2h[:, h, :], bank(b)[:, 0:T], ACT.Copy)
                elif kind == "moba":
                    r = slice(64 * (h % 2), 64 * (h % 2) + 64)
                    ins = act.activation(y5h[r, h // 2, :], bank(b)[r, 0:T], ACT.Copy)
                else:
                    ins = act.activation(y5h[:, 2 * h:2 * h + 2, :], bank(b).rearrange("p (a b) -> p a b", a=2), ACT.Copy)
                ins.then_inc(act_done, 1)

            def z_e(h):
                act.wait_ge(pe_done, at("z_s", h))
                if h:
                    act.wait_ge(pe_done, at("z_o", h - 1))
                else:
                    act.wait_ge(pe_done, at("pv", "fox", NH - 1))
                f = float(HD) ** -0.5
                n = T + P
                act.activation(S1[:, 0:n], bank(6)[:, 0:n], ACT.Copy, scale=f)
                link(act.activation(PT1[:, 0:n], bank(6)[:, 0:n], ACT.Abs, scale=f))
                link(act.activation(PT1[:, 0:n], PT1[:, 0:n], ACT.Exp, scale=-1.0))
                act.activation(PT1[:, 0:n], PT1[:, 0:n], ACT.Ln, bias=1.0).then_inc(act_done, 1)

            def z_x(h):
                act.wait_ge(dve_done, at("z_w", h))
                act.activation(S1[:, 0:T + P], S1[:, 0:T + P], ACT.Exp).then_inc(act_done, 1)

            def z_oc(h):
                act.wait_ge(pe_done, at("z_o", h))
                act.activation(sq_[:, h, :], bank(6)[:, 0:T], ACT.Copy).then_inc(act_done, 1)

            def yh(br):
                act.wait_ge(pe_done, at("z_o", NH - 1))
                act.wait_ge(dve_done, at("hn_mul", "fk1"))
                if br == 1:
                    act.wait_ge(dve_done, at("hn_mul", "go1"))
                act.activation(ybh[br][:, :, :], (fq_, gq_, sq_)[br][:, :, :], ACT.Copy).then_inc(act_done, 1)

            def mixh(q):
                act.wait_ge(dve_done, at("mix", q))
                act.activation(xh[:, 2 * q:2 * q + 2, :], gates[:, 2 * q:2 * q + 2, :], ACT.Copy).then_inc(act_done, 1)

            def ca(i):
                cg, cu = pair(0, i)
                act.wait_ge(pe_done, at("mm", cu, 1))
                if i >= 2:
                    act.wait_ge(dve_done, at("fm", 0, i - 2))
                for a, c in enumerate((cg, cu)):
                    for m in range(2):
                        f = a * KF + 2 * i + m
                        ins = act.activation(CA[i % 2][:, a, m * T:(m + 1) * T], bank(chunks[c]["banks"][0])[:, m * T:(m + 1) * T],
                                             ACT.Identity, scale=pcolumn("ffn_conv", 2 * 2 * KF + f), bias=pcolumn("ffn_conv_b", f))
                ins.then_inc(act_done, 1)

            def fs(f, i):
                cg, cu = pair(f, i)
                if i >= 2:
                    act.wait_ge(dve_done, at("fl", f, i - 2))
                if f == 0:
                    act.wait_ge(dve_done, at("cd", i))
                    ins = act.activation(SG[i % 2][:, :], CA[i % 2][:, 0, :], ACT.Silu)
                else:
                    act.wait_ge(pe_done, at("mm", cg, 1))
                    ins = act.activation(SG[i % 2][:, :], bank(chunks[cg]["banks"][0]), ACT.Silu)
                ins.then_inc(act_done, 1)

            def fh(f, i):
                act.wait_ge(dve_done, at("fm", f, i))
                act.activation(hh[:, 2 * i:2 * i + 2, :], mat(SG[i % 2]), ACT.Copy).then_inc(act_done, 1)

            def post1(c):
                act.wait_ge(dve_done, at("post0", c))
                link(act.activation(rn, ms, ACT.Ln, bias=eps))
                act.activation(rn, rn, ACT.Exp, scale=-0.5).then_inc(act_done, 1)

            def pl_h(g):
                act.wait_ge(pe_done, at("pl_mm", g))
                act.activation(y5h[:, 4 + g, :], bank(4 + g)[:, 0:T], ACT.Copy, scale=pcolumn("pool_scale_2", g)).then_inc(act_done, 1)

            run(act, "act", locals())

        @block.vector
        def _(dve):
            linked = [0]

            def link(ins):
                linked[0] += 1
                ins.then_inc(dve_link, 1)
                dve.wait_ge(dve_link, linked[0])

            def lo(c):
                dve.wait_ge(act_done, at("hi", c))
                dve.tensor_tensor(wlo[c % RING][:, :], raw[c % RING][:, :], whi[c % RING][:, :], ALU.subtract).then_inc(dve_done, 1)

            def params_c():
                dve.wait_ge(pe_done, at("params"))
                dve.tensor_copy(pcol[:, 0:n_first], bank(4)[:, 0:n_first])
                link(dve.tensor_copy(pcol[:, P:n_cols], bank(4)[:, P:n_cols]))
                dve.tensor_scalar(gsc, pcolumn("fox_qnorm"), float(HD) ** -0.5, None, ALU.mult).then_inc(dve_done, 1)

            def mean_square(src):
                for t in range(NT):
                    for i in range(2):
                        ins = dve.bn_stats(bst[:, t, 6 * i:6 * i + 6], src(t, i))
                link(ins)
                for t in range(NT):
                    ins = dve.bn_aggr(mv[:, t, 0:2], bst[:, t, :])
                link(ins)
                for t in range(NT):
                    ins = dve.scalar_tensor_tensor(ms[:, t:t + 1], mv[:, t, 0:1], mv[:, t, 0:1], mv[:, t, 1:2], ALU.mult, ALU.add)
                return ins

            def ns(name):
                src = NORM[name][0]
                if name == "norm_mix":
                    dve.wait_ge(x_in, 16)
                elif name == "norm_mem":
                    dve.wait_ge(mem_in, 16)
                elif name == "mem_g_2":
                    dve.wait_ge(mem2_in, 16)
                mean_square(lambda t, i: src[:, t, 512 * i:512 * i + 512]).then_inc(dve_done, 1)

            def nd(name):
                dve.wait_ge(act_done, at("nr", name))
                for t in range(NT):
                    ins = dve.tensor_scalar(diag[:, t, :], ident[:, :], rn[:, t:t + 1], None, ALU.mult)
                ins.then_inc(dve_done, 1)

            def nl(name, j):
                dve.wait_ge(act_done, at("nh", name, j))
                _, h_, l_ = NORM[name]
                for k in range(2):
                    kt = 2 * j + k
                    ins = dve.scalar_tensor_tensor(l_[:, kt, :], bank(j)[:, k * T:(k + 1) * T], pcolumn(name, kt), h_[:, kt, :],
                                                   ALU.mult, ALU.subtract)
                ins.then_inc(dve_done, 1)

            def rows1():
                dve.wait_ge(pe_done, at("mm", 0, 1))
                dve.wait_ge(par_in, 16 * N_PAR)
                dve.tensor_scalar(W2[:, 0, :], bank(0)[0:4, 0:T], fbias, -1.0, ALU.add, ALU.mult)
                dve.tensor_scalar(W2[:, 1, :], bank(1)[0:4, 0:T], dtb, None, ALU.add)
                dve.tensor_copy(GBR, bank(0)[0:4, T:2 * T]).then_inc(dve_done, 1)

            def rows3():
                dve.wait_ge(act_done, at("rows2"))
                link(dve.tensor_scalar(EBR, EBR, 1.0, None, ALU.add))
                dve.reciprocal(BETA, EBR)
                link(dve.scalar_tensor_tensor(SP2, W2, 0.0, E2, ALU.max, ALU.add))
                dve.tensor_scalar(SP2[:, 0, :], SP2[:, 0, :], -1.0, None, ALU.mult)
                link(dve.tensor_scalar(GLOG, SP2[:, 1, :], ealog, -1.0, ALU.mult, ALU.mult))
                one = ones[0:4, 0:1]
                dve.tensor_tensor_scan(cf[:, :], one.to_broadcast([4, T]), SP2[:, 0, :], 0.0, ALU.mult, ALU.add)
                for j in range(T // CH):
                    s = slice(j * CH, (j + 1) * CH)
                    ins = dve.tensor_tensor_scan(gc[:, s], one.to_broadcast([4, CH]), GLOG[:, s], 0.0, ALU.mult, ALU.add)
                link(ins)
                dve.tensor_scalar(ncf[:, :], cf[:, :], -1.0, None, ALU.mult)
                dve.tensor_scalar(ngc[:, :], gc[:, :], -1.0, None, ALU.mult)
                gcv = gc[:, :].rearrange("h (j c) -> h j c", c=CH)
                dve.tensor_tensor(TAIL.rearrange("h (j c) -> h j c", c=CH), gcv[:, :, CH - 1:CH].to_broadcast([4, T // CH, CH]), gcv,
                                  ALU.subtract).then_inc(dve_done, 1)

            def rows5():
                dve.wait_ge(act_done, at("rows4"))
                dve.tensor_tensor(BEGC, BETA, EGC, ALU.mult).then_inc(dve_done, 1)

            def rows7():
                dve.wait_ge(pe_done, at("rows6"))
                dve.memset(gS[:, :, :], 0.0)
                dve.tensor_copy(gcols[:, :, :, :].rearrange("p a b c -> p (a b c)"), bank(4)[:, 0:24]).then_inc(dve_done, 1)

            def cv_add(c):
                i = chunks[c]["i"]
                dve.wait_ge(act_done, at("cv_mul", c))
                dst = (gq_, gk_, gv_)[i // 2]
                for s in (1, 2, 3):
                    for m in range(2):
                        d = dst[:, 2 * (i % 2) + m, s:T]
                        ins = dve.scalar_tensor_tensor(d, bank(chunks[c]["banks"][0])[:, m * T:(m + 1) * T - s],
                                                       pcolumn("gdn_conv", (3 - s) * 12 + 2 * i + m), d, ALU.mult, ALU.add)
                    if s < 3:
                        link(ins)
                ins.then_inc(dve_done, 1)

            def hn_mul(job):
                dst, sq, rr, b, g, inv, f, gate = HN[job]
                dve.wait_ge(act_done, at("hn_r", job))
                ins = dve.scalar_tensor_tensor(dst, dst, g if g is not None else f, mat(rr), ALU.mult, ALU.mult)
                if gate is not None:
                    dve.wait_ge(act_done, at("copy", chunk_of("gz", 1)))
                    link(ins)
                    ins = dve.tensor_tensor(dst, dst, gate, ALU.mult)
                ins.then_inc(dve_done, 1)

            def g_mask(t):
                dve.wait_ge(pe_done, at("g_dec", t))
                for b, dst, m in ((4, gM, gda), (5, gAT, gdat)):
                    ins = dve.tensor_tensor(dst[:, :, :], per_head(bank(b)), m[:, :].unsqueeze(1).to_broadcast([P, NH, P]), ALU.add)
                ins.then_inc(dve_done, 1)

            def g_m(t):
                dve.wait_ge(pe_done, at("g_kk", t))
                dve.wait_ge(act_done, at("g_exp", t))
                dve.wait_ge(dve_done, at("rows7"))
                dve.tensor_tensor(gAT[:, :, :], per_head(bank(5)), gAT[:, :, :], ALU.mult)
                link(dve.tensor_tensor(gM[:, :, :], per_head(bank(4)), gM[:, :, :], ALU.mult))
                for h in range(NH):
                    ins = dve.scalar_tensor_tensor(gM[:, h, :], gM[:, h, :], gcols[:, t, 0, h:h + 1], strict[:, :], ALU.mult, ALU.mult)
                ins.then_inc(dve_done, 1)

            def g_vb(t):
                dve.wait_ge(pe_done, at("g_turn", t))
                for h in range(NH):
                    ins = dve.tensor_scalar(gVb[:, h, :], bank(5)[:, h * P:(h + 1) * P], gcols[:, t, 0, h:h + 1], None, ALU.mult)
                ins.then_inc(dve_done, 1)

            def l_upd(t, l):
                dve.wait_ge(pe_done, at("l_x", t, l))
                dve.wait_ge(pool_done, at("g_eye", t))
                if l < 5:
                    dve.tensor_tensor(gX[:, :, :], gX[:, :, :], per_head(bank(5)), ALU.subtract)
                dve.tensor_tensor(gY[:, :, :], gY[:, :, :], per_head(bank(4)), ALU.subtract).then_inc(dve_done, 1)

            def g_u(t):
                dve.wait_ge(pe_done, at("g_uw", t))
                dve.wait_ge(pool_done, at("l_mask", t, 5))
                dve.tensor_copy(gM[:, :, :], per_head(bank(4))).then_inc(dve_done, 1)

            def g_qg(t):
                dve.wait_ge(act_done, at("g_egc", t))
                s = slice(t * P, (t + 1) * P)
                dve.tensor_tensor(gq_[:, :, s], gq_[:, :, s], gX[:, :, :], ALU.mult).then_inc(dve_done, 1)

            def r_vn(t, j):
                r = slice(j * CH, (j + 1) * CH)
                dve.wait_ge(pe_done, at("r_ws", t, j))
                dve.tensor_tensor(gMs0[r, :, :], gM[r, :, :], per_head(banks[r, 4, :]), ALU.subtract).then_inc(dve_done, 1)

            def r_s(t, j):
                dve.wait_ge(pe_done, at("r_o", t, j))
                last = (j + 1) * CH - 1
                for h in range(NH):
                    ins = dve.scalar_tensor_tensor(gS[:, h, :], gS[:, h, :], gX[:, h, last:last + 1], bank(4)[:, h * P:(h + 1) * P],
                                                   ALU.mult, ALU.add)
                ins.then_inc(dve_done, 1)

            def sm(kind, h):
                s_, pt_, b, b2, nm, rs, rc = lane(kind, h)
                dve.wait_ge(pe_done, at("sc", kind, h))
                if before(kind, h) is not None:
                    dve.wait_ge(pe_done, at("pt", kind, before(kind, h)))
                v = bank(b).rearrange("p (t k) -> p t k", t=NT)
                if kind == "fox":
                    link(dve.tensor_tensor(mat(s_), v, cmask[:, :, :], ALU.add))
                    v = mat(s_)
                elif kind == "moba":
                    dve.wait_ge(pool_done, at("pool_tables"))
                    link(dve.scalar_tensor_tensor(mat(s_), dist[:, :, :], -SLOPE[h] / FACTOR[kind], v, ALU.mult, ALU.add))
                    v = mat(s_)
                ins = dve.tensor_reduce(nm, v, AX_X, ALU.max, negate=True)
                if FACTOR[kind] != 1.0:
                    link(ins)
                    ins = dve.tensor_scalar(nm, nm, FACTOR[kind], None, ALU.mult)
                ins.then_inc(dve_done, 1)

            def pn(kind, h):
                s_, pt_, b, b2, nm, rs, rc = lane(kind, h)
                dve.wait_ge(act_done, at("ex", kind, h))
                link(dve.reciprocal(rc, rs))
                for t in range(NT):
                    ins = dve.tensor_scalar(s_[:, t * T:(t + 1) * T], s_[:, t * T:(t + 1) * T], rc[:, t:t + 1], None, ALU.mult)
                ins.then_inc(dve_done, 1)

            def ol(kind, h):
                s_, pt_, b, *_ = lane(kind, h)
                dve.wait_ge(act_done, at("oc", kind, h))
                if kind == "mem":
                    o, i, hi_ = y2l[:, h, :], bank(b)[:, 0:T], y2h[:, h, :]
                elif kind == "moba":
                    r = slice(64 * (h % 2), 64 * (h % 2) + 64)
                    o, i, hi_ = y5l[r, h // 2, :], banks[r, b, 0:T], y5h[r, h // 2, :]
                else:
                    o, i, hi_ = y5l[:, 2 * h:2 * h + 2, :], bank(b).rearrange("p (a b) -> p a b", a=2), y5h[:, 2 * h:2 * h + 2, :]
                dve.tensor_tensor(o, i, hi_, ALU.subtract).then_inc(dve_done, 1)

            def z_lk(h):
                dve.wait_ge(act_done, at("z_e", h))
                n = T + P
                if h:
                    dve.wait_ge(pe_done, at("z_rc", h - 1))
                link(dve.scalar_tensor_tensor(PT1[:, 0:n], S1[:, 0:n], 0.0, PT1[:, 0:n], ALU.max, ALU.add))
                link(dve.tensor_scalar(PT1[:, 0:n], PT1[:, 0:n], -1.0, None, ALU.mult))
                for o in (0, T):
                    ins = dve.tensor_tensor(PT1[:, o:o + P], PT1[:, o:o + P], sbm[:, :], ALU.mult)
                ins.then_inc(dve_done, 1)

            def z_w(h):
                dve.wait_ge(pe_done, at("z_rc", h))
                n = T + P
                link(dve.tensor_tensor(S1[:, 0:n], S1[:, 0:n], bank(7)[:, 0:n], ALU.add))
                for o in (0, T):
                    ins = dve.tensor_tensor(S1[:, o:o + P], S1[:, o:o + P], sba[:, :], ALU.add)
                ins.then_inc(dve_done, 1)

            def yl_(br):
                dve.wait_ge(act_done, at("yh", br))
                dve.tensor_tensor(ybl[br][:, :, :], (fq_, gq_, sq_)[br][:, :, :], ybh[br][:, :, :], ALU.subtract).then_inc(dve_done, 1)

            def gated(c):
                ch = chunks[c]
                dve.wait_ge(pe_done, at("mm", c, 1))
                dve.wait_ge(act_done, at("copy", chunk_of("gate", 11)))
                for q in range(2):
                    g = gates[:, 8 * ch["br"] + 4 * ch["i"] + 2 * q:8 * ch["br"] + 4 * ch["i"] + 2 * q + 2, :]
                    ins = dve.tensor_tensor(g, g, bank(ch["banks"][q]).rearrange("p (a b) -> p a b", a=2), ALU.mult)
                ins.then_inc(dve_done, 1)

            def mix(q):
                g = [gates[:, 8 * br + 2 * q:8 * br + 2 * q + 2, :] for br in range(3)]
                link(dve.tensor_tensor(g[0], g[0], g[1], ALU.add))
                dve.tensor_tensor(g[0], g[0], g[2], ALU.add).then_inc(dve_done, 1)

            def mixl(q):
                dve.wait_ge(act_done, at("mixh", q))
                dve.tensor_tensor(xl[:, 2 * q:2 * q + 2, :], gates[:, 2 * q:2 * q + 2, :], xh[:, 2 * q:2 * q + 2, :],
                                  ALU.subtract).then_inc(dve_done, 1)

            def resid(c):
                dve.wait_ge(pe_done, at("mm", c, 1))
                for t in range(NT):
                    for nb in range(2):
                        s = x[:, t, 512 * nb:512 * nb + 512]
                        ins = dve.tensor_tensor(s, s, bank(4 + 2 * t + nb), ALU.add)
                ins.then_inc(dve_done, 1)

            def post0(c):
                dve.wait_ge(pe_done, at("mm", c, 1))
                mean_square(lambda t, i: bank(4 + 2 * t + i)).then_inc(dve_done, 1)

            def post2(c):
                dve.wait_ge(act_done, at("post1", c))
                dve.wait_ge(gains_in, 16 * (POSTS.index(c) + 1))
                f = 0.5 if chunks[c]["name"] in ("ffn1_w_down_2", "ffn2_w_down_2") else 1.0
                tmp = pin_tmp(c)
                for t in range(NT):
                    for nb in range(2):
                        s = x[:, t, 512 * nb:512 * nb + 512]
                        d = tmp[(2 * t + nb) % 2]
                        link(dve.scalar_tensor_tensor(d, bank(4 + 2 * t + nb), rn[:, t:t + 1], gain[:, 512 * nb:512 * nb + 512],
                                                      ALU.mult, ALU.mult))
                        ins = dve.scalar_tensor_tensor(s, d, f, s, ALU.mult, ALU.add)
                        if (t, nb) != (1, 1):
                            link(ins)
                ins.then_inc(dve_done, 1)

            def cd(i):
                dve.wait_ge(act_done, at("ca", i))
                for s in (1, 2):
                    for a, c in enumerate(pair(0, i)):
                        for m in range(2):
                            d = CA[i % 2][:, a, m * T + s:(m + 1) * T]
                            ins = dve.scalar_tensor_tensor(d, bank(chunks[c]["banks"][0])[:, m * T:(m + 1) * T - s],
                                                           pcolumn("ffn_conv", (2 - s) * 2 * KF + a * KF + 2 * i + m), d,
                                                           ALU.mult, ALU.add)
                    if s == 1:
                        link(ins)
                ins.then_inc(dve_done, 1)

            def fm(f, i):
                dve.wait_ge(act_done, at("fs", f, i))
                if f == 0:
                    other = CA[i % 2][:, 1, :]
                else:
                    other = bank(chunks[pair(f, i)[1]]["banks"][0])
                    dve.wait_ge(pe_done, at("mm", pair(f, i)[1], 1))
                dve.tensor_tensor(SG[i % 2][:, :], SG[i % 2][:, :], other, ALU.mult).then_inc(dve_done, 1)

            def fl(f, i):
                dve.wait_ge(act_done, at("fh", f, i))
                dve.tensor_tensor(hl[:, 2 * i:2 * i + 2, :], mat(SG[i % 2]), hh[:, 2 * i:2 * i + 2, :], ALU.subtract).then_inc(dve_done, 1)

            def pl_win(g):
                dve.wait_ge(act_done, at("copy", chunk_of("pin", 1)))
                dve.wait_ge(pool_done, at("pool_tables"))
                cur = pin[:, g, :]
                if g == 0:
                    link(dve.reciprocal(rcnt.rearrange("p g t -> p (g t)"), rcnt.rearrange("p g t -> p (g t)")))
                for l in range(g + 1):
                    s, nxt = 1 << l, win[:, l % 2, :]
                    dve.tensor_copy(nxt[:, 0:s], cur[:, 0:s])
                    link(dve.tensor_tensor(nxt[:, s:T], cur[:, s:T], cur[:, 0:T - s], ALU.add))
                    cur = nxt
                link(dve.tensor_tensor(cur, cur, rcnt[:, g, :], ALU.mult))
                dve.tensor_tensor(pin[:, g, :], cur, pin[:, g, :], ALU.subtract).then_inc(dve_done, 1)

            def pl_l(g):
                dve.wait_ge(act_done, at("pl_h", g))
                dve.scalar_tensor_tensor(y5l[:, 4 + g, :], bank(4 + g)[:, 0:T], pcolumn("pool_scale_2", g), y5h[:, 4 + g, :],
                                         ALU.mult, ALU.subtract).then_inc(dve_done, 1)

            steps = dict(locals())
            steps["yl"] = yl_
            run(dve, "dve", steps)


def kernel(**inputs):
    import concourse.bacc as bacc
    from concourse.bass_utils import run_bass_kernel_spmd

    nc = bacc.Bacc("TRN2", target_bir_lowering=False, num_devices=1)
    arrays, w = {}, {}
    for name, a in inputs.items():
        a = np.asarray(a)
        a = a.reshape(-1, a.shape[-1])
        a = np.ascontiguousarray(a)
        arrays[f"in_{name}"] = a
        w[name] = nc.dram_tensor(f"in_{name}", a.shape, mybir.dt.from_np(a.dtype), kind="ExternalInput").ap()
    out = nc.dram_tensor("out", (T, D), F32, kind="ExternalOutput").ap()
    two_blocks_kernel(nc, w, out)
    r = run_bass_kernel_spmd(nc, [arrays], core_ids=[0])
    return r.results[0]["out"].reshape(1, T, D)
```

```python
from contextlib import ExitStack

import numpy as np

import concourse.bass as bass
from concourse import mybir

F32 = mybir.dt.float32
F32R = mybir.dt.float32r
ALU = mybir.AluOpType
ACT = mybir.ActivationFunctionType
AX_X = mybir.AxisListType.X

P = 128
T = 256
NT = T // P
D = 1024
KD = D // P
HD = 128
NH = 4
DFF = 2816
KF = DFF // P
EPS = 1e-6
NEG = -1e30
CH = 64

RING = 3
LEAD = 2
BRANCHES = (2, 0, 1)

FQ, FK, FV, FF = 0, 512, 1024, 1536
GQ = 1540
GB = GQ + 3 * 512
GA = GB + 4
GZ = GA + 4
SQ = GZ + 512
SK, SV = SQ + 512, SQ + 1024
GATES = SQ + 3 * 512


def param_columns():
    col, n = {}, 0
    for name, rows in [("norm_mix", 8), ("norm_xq", 8), ("norm_mem", 8), ("norm_ffn", 8), ("ffn1_pre_g_2", 8),
                       ("mix_pre_g_2", 8), ("xa_pre_g_2", 8), ("mem_g_2", 8), ("ffn2_pre_g_2", 8),
                       ("gdn_conv", 48), ("fox_qnorm", 1), ("fox_knorm", 1), ("gdn_onorm", 1),
                       ("mq_norm", 1), ("mk_norm", 1)]:
        col[name] = n
        n += rows
    first = n
    n = 128
    for name, rows in [("ffn_conv", 3 * 2 * KF), ("ffn_conv_b", 2 * KF), ("gate_bias", 24), ("pool_scale_2", 4)]:
        col[name] = n
        n += rows
    return col, first, n


class Plan:

    def __init__(self):
        self.steps, self.number, self.engine = [], {}, {}
        self.count = {"pe": 0, "act": 0, "dve": 0, "pool": 0}
        self.chunks, self.bank_read, self.bank_wait, self.ready, self.fresh = [], {}, {}, {}, {}

    def add(self, engine, name, *args):
        self.count[engine] += 1
        self.steps.append((engine, name, args))
        self.number[(name, *args)] = self.count[engine]
        self.engine[name] = engine

    def take(self, user, banks, reader):
        self.bank_wait[user] = [r for r in dict.fromkeys(self.bank_read.get(b) for b in banks) if r]
        for b in banks:
            self.bank_read[b] = reader


def build_chunks(w):
    out = []

    def kpn(a):
        return a.rearrange("(k p) n -> p k n", p=P)

    def cols(name, c0, x, banks, evac, **k):
        out.append(dict(kind="A", srcs=[((0, 256), kpn(w[name][:, c0:c0 + 256]))], x=x, banks=banks, evac=evac, **k))

    def vals(name, c0, x, evac, **k):
        for half in range(2):
            out.append(dict(kind="V", half=half, srcs=[((0, 512), kpn(w[name][512 * half:512 * half + 512, c0:c0 + 512]))],
                            x=x, banks=(2, 3), evac=evac if half else None, **k))

    def rows(name, n, x, evac):
        for j in range(n):
            out.append(dict(kind="R", j=j, last=j == n - 1, srcs=[((0, 1024), kpn(w[name][256 * j:256 * j + 256, :]))],
                            x=x, banks=(4, 5, 6, 7), evac=evac if j == n - 1 else None, name=name))

    win = "w_in"
    turn = 0
    for i in range(6):
        cols(win, GQ + 256 * i, "x", (turn % 2,), "conv", i=i)
        turn += 1
    out.append(dict(kind="S", srcs=[((0, 8), kpn(w[win][:, GB:GB + 8])), ((8, 12), kpn(w[win][:, FF:FF + 4])),
                                    ((12, P), kpn(w[win][:, GZ:GZ + P - 12]))], x="x", banks=(0,), evac="rows"))
    turn += 1
    for what, c0 in (("fq", FQ), ("fk", FK)):
        for i in range(2):
            cols(win, c0 + 256 * i, "x", (turn % 2,), "copy", to=what, i=i)
            turn += 1
    vals(win, FV, "x", "vcopy", to="fv")
    for what, c0 in (("sq", SQ), ("sk", SK)):
        for i in range(2):
            cols(win, c0 + 256 * i, "x", (turn % 2,), "copy", to=what, i=i)
            turn += 1
    vals(win, SV, "x", "vcopy", to="sv")
    for i in range(2):
        cols(win, GZ + 256 * i, "x", (turn % 2,), "gz", i=i)
        turn += 1
    for i in range(12):
        cols(win, GATES + 256 * i, "x", (turn % 2,), "gate", i=i)
        turn += 1
    for br in BRANCHES:
        name = ("w_oa", "w_ob", "w_oc")[br]
        for i in range(2):
            out.append(dict(kind="O", srcs=[((0, 512), kpn(w[name][:, 512 * i:512 * i + 512]))], x="y%d" % br, br=br,
                            i=i, banks=(2 * i, 2 * i + 1), evac="gated"))
    rows("w_out", 4, "x", "resid")
    for i in range(2):
        cols("w_mkv", 256 * i, "m1", (i,), "copy", to="mk", i=i)
    for i in range(2):
        cols("w_mq", 256 * i, "x", (i,), "copy", to="mq", i=i)
    vals("w_mkv", 512, "m1", "vcopy", to="mv")

    def xa_k(i):
        cols("xa_wkv_2", 256 * i, "m2", (i % 2,), "copy", to="xk", i=i)

    def xa_v(i):
        vals("xa_wkv_2", 1024 + 512 * i, "m2", "vcopy", to="xv%d" % i)

    xa_k(0)
    xa_k(1)
    rows("w_mo", 2, "ym", "resid")
    xa_k(2)

    def ffn(f, gate, up, down, c_up):
        for i in range(KF // 2):
            b = 2 * ((KF // 2 - 1 - i) % 4)
            cols(gate, 256 * i, "x", (b,), None, f=f, i=i, part="gate")
            cols(up, c_up + 256 * i, "x", (b + 1,), "ffn", f=f, i=i, part="up")
        rows(down, KF // 2, "h%d" % f, "resid" if f == 0 else "post")

    ffn(0, "w_up", "w_up", "w_down", DFF)
    xa_k(3)
    ffn(1, "ffn1_w_gate_2", "ffn1_w_up_2", "ffn1_w_down_2", 0)
    xa_v(0)
    win = "w_in_2"
    vals(win, 1024, "x", "vcopy", to="bv")
    for n, i in enumerate((0, 2, 1, 3)):
        cols(win, 256 * i, "x", (n % 2,), "copy", to="qk", i=i)
    for i in range(2):
        cols(win, 1536 + 256 * i, "x", (i % 2,), "copy", to="pin", i=i)
    rows("w_out_2", 4, "y5", "post")
    xa_v(1)
    for i in range(4):
        cols("xa_wq_2", 256 * i, "x", (i % 2,), "copy", to="xq", i=i)
    rows("xa_wo_2", 4, "y5", "post")
    ffn(2, "ffn2_w_gate_2", "ffn2_w_up_2", "ffn2_w_down_2", 0)
    for c in out:
        c.setdefault("name", "")
    return out


def build_plan(chunks):
    pl = Plan()
    pl.chunks = chunks
    n = len(chunks)
    side, late = [], []
    ready = {f"y{br}": [("yl", br)] for br in range(3)}
    ready["ym"] = [("ol", "mem", 2), ("ol", "mem", 3)]

    def hook():
        links = [chain.pop(0) for chain in side if chain]
        for i in range(max((len(link_) for link_ in links), default=0)):
            for link_ in links:
                if i < len(link_):
                    place(link_[i])
        side[:] = [chain for chain in side if chain]

    def place(s):
        if callable(s):
            s()
        else:
            pl.add(*s)

    def drain():
        while side:
            hook()

    def split(c):
        if c < n:
            pl.add("act", "hi", c)
            pl.add("dve", "lo", c)

    def mm(c):
        ch = chunks[c]
        if ch["x"][0] == "h":
            pl.ready[c] = [("fl", int(ch["x"][1]), ch["j"])]
        elif ch["x"] in ("x", "m1", "m2"):
            pl.ready[c], pl.fresh[c] = [], ready[ch["x"]]
            if ch["kind"] != "V" or ch["half"]:
                ready[ch["x"]] = None
        else:
            pl.ready[c] = ready[ch["x"]]
        split(c + LEAD)
        ev = ch["evac"]
        end = {"conv": ("cv_add", c), "copy": ("copy", c), "vcopy": ("copy", c), "gz": ("copy", c), "gate": ("copy", c),
               "rows": ("rows0",), "gated": ("gated", c), "resid": ("resid", c), "post": ("post2", c)}
        if ch["kind"] in "AOS":
            if "f" in ch:
                reader = ("cd", ch["i"]) if ch["f"] == 0 else ("fm" if ch["part"] == "up" else "fs", ch["f"], ch["i"])
            else:
                reader = end[ev]
            pl.take(("mm", c, 0), ch["banks"], reader)
        elif ch["kind"] == "V" and ch["half"] == 0:
            pl.take(("mm", c, 0), ch["banks"], ("copy", c + 1))
        elif ch["kind"] == "R" and ch["j"] == 0:
            e = c
            while not chunks[e]["last"]:
                e += 1
            pl.take(("mm", c, 0), ch["banks"], end[chunks[e]["evac"]][:1] + (e, 1))
        for s in late:
            pl.add(*s)
        late.clear()
        if ch["name"] in ("w_down", "ffn1_w_down_2", "ffn2_w_down_2") and ch["j"] == 1:
            pl.add("act", "tables", ch["name"])
        pl.add("pe", "mm", c, 0)
        hook()
        pl.add("pe", "mm", c, 1)
        if ev == "rows":
            pl.add("dve", "rows0")
        elif ev == "conv":
            pl.add("act", "cv_mul", c)
            pl.add("dve", "cv_add", c)
            late.append(("act", "cv_silu", c))
        elif ev in ("copy", "vcopy", "gz", "gate"):
            pl.add("act", "copy", c)
        elif ev == "gated":
            pl.add("dve", "gated", c)
        elif ev == "resid":
            for t in range(NT):
                pl.add("dve", "resid", c, t)
        elif ev == "post":
            for t in range(NT):
                pl.add("act", "post1", c, t)
                pl.add("dve", "post0", c, 1 - t)
            pl.add("act", "post_r", c)
            for t in range(NT):
                pl.add("dve", "post2", c, t)
        elif ev == "ffn":
            f, i = ch["f"], ch["i"]
            if f == 0:
                pl.add("act", "ca", i)
                pl.add("dve", "cd", i)
            rest = [("act", "fs", f, i), ("dve", "fm", f, i), ("act", "fh", f, i), ("dve", "fl", f, i)]
            if f == 0:
                late.extend(rest)
            else:
                for s in rest:
                    pl.add(*s)
        hook()

    def norm(name, into="x"):
        norm_scale(name)
        norm_turn(name, into)

    def norm_scale(name):
        for t in range(NT):
            pl.add("act", "ns", name, t)
        pl.add("act", "nr", name)
        for t in range(NT):
            pl.add("dve", "nd", name, t)

    def norm_turn(name, into="x"):
        for j in range(4):
            pl.take(("nt", name, j), (j,), ("nl", name, j))
            pl.add("pe", "nt", name, j)
            pl.add("act", "nh", name, j)
            pl.add("dve", "nl", name, j)

        ready[into] = ("nl", name)

    def hn(*jobs):
        links = [[("act", "hn_sq", jobs[0])]]
        for n, job in enumerate(jobs):
            links.append([("pe", "hn_sum", job), ("act", "hn_r", job), ("dve", "hn_mul", job)]
                         + [("act", "hn_sq", after) for after in jobs[n + 1:n + 2]])
        return links

    def gdn(t):
        c = [[("pe", "g_dec", t), ("dve", "g_mask", t), ("act", "g_exp", t)],
             [("pe", "g_kk", t), ("dve", "g_m", t), ("pool", "g_eye", t)],
             [("pe", "g_turn", t), ("act", "g_kb", t), ("dve", "g_vb", t)]]
        c += [[("pool", "l_mask", t, 0), ("pe", "l_u", t, 0), ("dve", "l_upd", t, 0)]]
        for l in range(1, 6):
            c += [[("pool", "l_mask", t, l), ("pe", "l_u", t, l), ("act", "l_uc", t, l)],
                  [("pe", "l_x", t, l), ("dve", "l_upd", t, l)]]
        c += [[("pe", "g_uw", t), ("dve", "g_u", t), ("act", "g_w", t)],
              [("pe", "g_bc", t), ("act", "g_egc", t), ("dve", "g_qg", t)]]
        for j in range(2):
            c += [[("pe", "r_ws", t, j), ("dve", "r_vn", t, j)],
                  [("pe", "r_o", t, j), ("act", "r_oc", t, j), ("dve", "r_s", t, j)]]
        return c

    def attend(kind, h):
        lane = kind, h
        return [[("pe", "sc", *lane), ("dve", "sm", *lane), ("act", "ex", *lane), ("dve", "pn", *lane)],
                [("pe", "pt", *lane), ("act", "pc", *lane)],
                [("pe", "pv", *lane), ("act", "oc", *lane)] + ([] if kind == "fox" else [("dve", "ol", *lane)])]

    def stick(h):
        return [[("pe", "z_s", h), ("act", "z_e", h), ("dve", "z_lk", h)],
                [("pe", "z_rc", h), ("dve", "z_w", h), ("act", "z_x", h)],
                [("pe", "z_o", h), ("act", "z_oc", h)]]

    pl.add("pool", "consts")
    pl.add("pe", "params")
    pl.add("dve", "params_c")
    split(0)
    split(1)
    norm("norm_mix")
    pl.add("pool", "consts2")
    c = 0
    for _ in range(7):
        mm(c)
        c += 1
    pl.add("act", "tables", "rows")
    a = [[("pe", "rows0p"), ("dve", "rows1")],
         [("act", "rows2"), ("dve", "rows3"), ("act", "rows4"), ("dve", "rows5")],
         [("pe", "rows6"), ("dve", "rows7")]]
    b = []
    a += hn("gq0", "gk0", "gq1", "gk1")
    for t in range(2):
        a += gdn(t)
    a += hn("go0", "go1")
    side.append(a)
    for _ in range(4):
        mm(c)
        c += 1
    b += hn("fq0", "fq1", "fk0", "fk1")
    side.append(b)
    mm(c)
    mm(c + 1)
    c += 2
    for h in range(NH):
        b += attend("fox", h)
    if not any(chain is b for chain in side):
        side.append(b)
    for _ in range(6):
        mm(c)
        c += 1
    for h in range(NH):
        b += stick(h)
    if not any(chain is b for chain in side):
        side.append(b)
    for _ in range(2):
        mm(c)
        c += 1
    pl.add("act", "gzs")
    for _ in range(12):
        mm(c)
        c += 1
    while b:
        hook()
    drain()
    for nth, br in enumerate(BRANCHES):
        if nth == 0:
            pl.add("act", "yh", br)
            pl.add("dve", "yl", br)
        pl.add("act", "gsig", br)
        mm(c)
        if nth < 2:
            pl.add("act", "yh", BRANCHES[nth + 1])
            pl.add("dve", "yl", BRANCHES[nth + 1])
        if nth == 1:
            mm(c + 1)
            pl.add("dve", "premix")
        elif nth == 2:
            pl.add("act", "tables", "blend")
            mm(c + 1)
        else:
            mm(c + 1)
        c += 2
    for q in range(4):
        pl.add("dve", "mix", q)
        pl.add("act", "mixh", q)
        pl.add("dve", "mixl", q)
    ready["x"] = ("mixl",)
    pl.add("pool", "mem_load")
    mm(c)
    mm(c + 1)
    mm(c + 2)
    norm_scale("norm_mem")
    side.append([[lambda: norm_turn("norm_mem", "m1")]])
    mm(c + 3)
    norm_scale("norm_xq")
    c += 4
    mm(c)
    mm(c + 1)
    c += 2
    norm_turn("norm_xq")
    side.append(hn("mk0", "mk1"))
    pl.add("pool", "mem2_load")
    for _ in range(2):
        mm(c)
        c += 1
    drain()
    side.append(hn("mq0", "mq1"))
    mm(c)
    norm_scale("mem_g_2")
    mm(c + 1)
    c += 2
    drain()
    norm_turn("mem_g_2", "m2")
    for lane in range(2):
        side.append(attend("mem", lane) + attend("mem", lane + 2))
    mm(c)
    mm(c + 1)
    c += 2
    drain()
    mm(c)
    mm(c + 1)
    c += 2
    norm_scale("norm_ffn")
    mm(c)
    c += 1
    norm_turn("norm_ffn")
    pl.add("pool", "gain_load", 0)
    for _ in range(KF + KF // 2):
        mm(c)
        c += 1
    norm_scale("ffn1_pre_g_2")
    mm(c)
    c += 1
    norm_turn("ffn1_pre_g_2")
    for _ in range(KF + KF // 2):
        mm(c)
        c += 1
    pl.add("pool", "gain_load", 1)
    norm_scale("mix_pre_g_2")
    mm(c)
    mm(c + 1)
    c += 2
    norm_turn("mix_pre_g_2")
    pl.add("pool", "pool_tables")
    for _ in range(4):
        mm(c)
        c += 1
    for lane in range(2):
        side.append(sum((attend("moba", h) for h in range(lane, 8, 2)), []))
    for _ in range(4):
        mm(c)
        c += 1
    for g in range(4):
        pl.add("dve", "pl_win", g)
        hook()
    drain()
    for g in range(4):
        pl.add("pe", "pl_mm", g)
        pl.add("act", "pl_h", g)
        pl.add("dve", "pl_l", g)
    ready["y5"] = [("ol", "moba", 6), ("ol", "moba", 7), ("pl_l", 3)]
    for _ in range(4):
        mm(c)
        c += 1
    pl.add("pool", "gain_load", 2)
    norm_scale("xa_pre_g_2")
    mm(c)
    mm(c + 1)
    c += 2
    norm_turn("xa_pre_g_2")
    for i in range(4):
        mm(c)
        c += 1
        if i < 2:
            side.append(attend("xa", i) + attend("xa", i + 2))
    drain()
    ready["y5"] = [("ol", "xa", 2), ("ol", "xa", 3)]
    for _ in range(4):
        mm(c)
        c += 1
    pl.add("pool", "gain_load", 3)
    norm("ffn2_pre_g_2")
    for _ in range(KF + KF // 2):
        mm(c)
        c += 1
    assert c == n, (c, n)
    return pl


def two_blocks_kernel(nc, w, out):
    chunks = build_chunks(w)
    plan = build_plan(chunks)
    COL, n_first, n_cols = param_columns()

    with ExitStack() as fixed:
        def sb(name, shape, dt=F32, stack=fixed):
            return stack.enter_context(nc.sbuf_tensor(name, shape, dt))

        raw = [sb(f"raw{i}", [P, 2048]) for i in range(RING)]
        whi = [sb(f"whi{i}", [P, 2048], F32R) for i in range(RING)]
        wlo = [sb(f"wlo{i}", [P, 2048], F32R) for i in range(RING)]
        x = sb("x_tok", [P, NT, D])
        xh = sb("xh", [P, KD, T], F32R)
        xl = sb("xl", [P, KD, T], F32R)
        ident = sb("ident", [P, P])
        ones = sb("ones", [P, P])
        cmask = sb("cmask", [P, NT, T])
        pcol = sb("pcol", [P, 3 * P])
        small = sb("small", [P, 64])
        eps = small[:, 0:1]
        ms = small[:, 32:34]
        rn = small[:, 34:36]
        fbias, alog, dtb, ealog = (small[0:4, 36 + i:37 + i] for i in range(4))
        per_gate = small[0:4, 36:39]
        gsc = small[:, 40:41]
        nmx = [small[:, 42:44], small[:, 44:46]]
        rsm = [small[:, 46:48], small[:, 48:50]]
        rrc = [small[:, 50:52], small[:, 52:54]]

        r1 = ExitStack()
        sbm = sb("sbm", [P, P], stack=r1)
        sba = sb("sba", [P, P], stack=r1)
        tri = sb("tri", [P, P], stack=r1)
        gda = sb("gda", [P, P], stack=r1)
        gdat = sb("gdat", [P, P], stack=r1)
        strict = sb("strict", [P, P], stack=r1)
        lev = sb("lev", [P, 6, P], stack=r1)
        sel = sb("sel", [4, NH, T], stack=r1)
        cf = sb("cf", [4, T], stack=r1)
        ncf = sb("ncf", [4, T], stack=r1)
        gc = sb("gc", [4, T], stack=r1)
        ngc = sb("ngc", [4, T], stack=r1)
        gcols = sb("gcols", [P, NT, 3, 4], stack=r1)
        sq_ = sb("sq_", [P, NH, T], stack=r1)
        fq_ = sb("fq_", [P, NH, T], stack=r1)
        gq_ = sb("gq_", [P, NH, T], stack=r1)
        gates = sb("gates", [P, 24, T], stack=r1)
        r1a = ExitStack()
        fk_ = sb("fk_", [P, NH, T], stack=r1a)
        sk_ = sb("sk_", [P, NH, T], stack=r1a)
        fv_ = sb("fv_", [P, NT, 512], stack=r1a)
        sv_ = sb("sv_", [P, NT, 512], stack=r1a)
        S1 = sb("S1", [P, 512], stack=r1a)
        PT1 = sb("PT1", [P, 512], stack=r1a)
        gk_ = sb("gk_", [P, NH, T], stack=r1a)
        gv_ = sb("gv_", [P, NH, T], stack=r1a)
        gz_ = sb("gz_", [P, NH, T], stack=r1a)
        gM, gAT, gX, gY, gU, gMs0, gMs1, gKb, gVb, gKt, gS = (
            sb(nm, [P, NH, P], stack=r1a) for nm in
            ("gM", "gAT", "gX", "gY", "gU", "gMs0", "gMs1", "gKb", "gVb", "gKt", "gS"))
        gMs = [gMs0, gMs1]
        r1a.close()
        r1b = ExitStack()
        ybh, ybl = {}, {}
        for br in (2, 0, 1):
            ybh[br] = sb(f"ybh{br}", [P, NH, T], F32R, stack=r1b)
            ybl[br] = sb(f"ybl{br}", [P, NH, T], F32R, stack=r1b)
        r1b.close()
        r1.close()
        r2p = ExitStack()
        xs = sb("xs", [P, NT, D], stack=r2p)
        gain = sb("gain", [P, D], stack=r2p)
        m2h = sb("m2h", [P, KD, T], F32R, stack=r2p)
        m2l = sb("m2l", [P, KD, T], F32R, stack=r2p)
        xk_ = sb("xk_", [P, KD, T], stack=r2p)
        xv_ = sb("xv_", [P, NT, D], stack=r2p)
        r2 = ExitStack()
        memx = sb("memx", [P, NT, D], stack=r2)
        mh = sb("mh", [P, KD, T], F32R, stack=r2)
        ml = sb("ml", [P, KD, T], F32R, stack=r2)
        mk_ = sb("mk_", [P, NH, T], stack=r2)
        mv_ = sb("mv_", [P, NT, 512], stack=r2)
        mq_ = sb("mq_", [P, NH, T], stack=r2)
        S2 = [sb(f"S2{i}", [P, 512], stack=r2) for i in range(2)]
        PT2 = [sb(f"PT2{i}", [P, 512], stack=r2) for i in range(2)]
        y2h = sb("y2h", [P, NH, T], F32R, stack=r2)
        y2l = sb("y2l", [P, NH, T], F32R, stack=r2)
        r2.close()
        r3 = ExitStack()
        hh = sb("hh", [P, KF, T], F32R, stack=r3)
        hl = sb("hl", [P, KF, T], F32R, stack=r3)
        CA = [sb(f"CA{i}", [P, 2, 512], stack=r3) for i in range(2)]
        SG = [sb(f"SG{i}", [P, 512], stack=r3) for i in range(2)]
        r3.close()
        r5 = ExitStack()
        pin = sb("pin", [P, 4, T], stack=r5)
        rcnt = sb("rcnt", [P, 4, T], stack=r5)
        qk_ = sb("qk_", [P, KD, T], stack=r5)
        bv_ = sb("bv_", [P, NT, 512], stack=r5)
        y5h = sb("y5h", [P, KD, T], F32R, stack=r5)
        y5l = sb("y5l", [P, KD, T], F32R, stack=r5)
        S5 = [sb(f"S5{i}", [P, 512], stack=r5) for i in range(2)]
        PT5 = [sb(f"PT5{i}", [P, 512], stack=r5) for i in range(2)]
        poolw = sb("poolw", [P, 4, P], stack=r5)
        win = sb("win", [P, 2, T], stack=r5)
        r5.close()
        r2p.close()
        dist = cmask

        banks = fixed.enter_context(nc.psum_tensor("banks", [P, 8, 512], F32))

        def bank(i):
            return banks[:, i, :]

        def sem(name):
            return fixed.enter_context(nc.semaphore(name))

        pe_done, act_done, dve_done, pool_done = (sem(s) for s in ("pe_done", "act_done", "dve_done", "pool_done"))
        DONE = {"pe": pe_done, "act": act_done, "dve": dve_done, "pool": pool_done}
        raw_in = [sem(f"raw_in{i}") for i in range(RING)]
        x_in, par_in, mem_in, mem2_in, gains_in, pw_in, out_done = (
            sem(s) for s in ("x_in", "par_in", "mem_in", "mem2_in", "gains_in", "pw_in", "out_done"))
        act_link, dve_link, pool_link = sem("act_link"), sem("dve_link"), sem("pool_link")

        def at(name, *args):
            return plan.number[(name, *args)]

        landed, used = [], [0] * RING
        for c, ch in enumerate(chunks):
            used[c % RING] += 16 * len(ch["srcs"])
            landed.append(used[c % RING])

        N_PAR = 2
        LOG_EXP = "natural_log_exp_and_others"
        last = {ch["name"]: c for c, ch in enumerate(chunks) if ch["kind"] == "R"}
        LAST_ROWS = {"norm_xq": last["w_out"], "norm_ffn": last["w_mo"], "ffn1_pre_g_2": last["w_down"],
                     "mix_pre_g_2": last["ffn1_w_down_2"], "xa_pre_g_2": last["w_out_2"], "ffn2_pre_g_2": last["xa_wo_2"]}
        NORM_BEFORE = {"norm_xq": "norm_mem", "mem_g_2": "norm_xq", "norm_ffn": "mem_g_2", "ffn1_pre_g_2": "norm_ffn"}
        LAST_NORM = {last["ffn1_w_down_2"]: "ffn1_pre_g_2", last["w_out_2"]: "mix_pre_g_2", last["xa_wo_2"]: "xa_pre_g_2",
                     last["ffn2_w_down_2"]: "ffn2_pre_g_2"}
        POSTS = [c for c, ch in enumerate(chunks) if ch["evac"] == "post"]

        def width(ch):
            return {"A": 256, "S": 256, "V": 512, "O": 512, "R": 1024}[ch["kind"]]

        def chunk_of(to, i):
            return max(c for c, ch in enumerate(chunks)
                       if (ch.get("to") == to or ch["evac"] == to) and (i is None or ch.get("i") == i))

        def pair(f, i):
            cg, cu = (c for c, ch in enumerate(chunks) if ch.get("f") == f and ch.get("i") == i)
            return cg, cu

        def run(e, engine, steps):
            n = 0
            for eng, name, args in plan.steps:
                if eng != engine:
                    continue
                if n and engine != "pe" and name not in ("hi", "lo"):
                    e.wait_ge(DONE[engine], n)
                steps[name](*args)
                n += 1

        def gate_row(i):
            return gates[0:4, i, :]

        W2, E2, GBR, EBR = gates[0:4, 0:2, :], gates[0:4, 2:4, :], gate_row(4), gate_row(5)
        SP2, BETA, GLOG, TAIL, ETAIL, EGC, BEGC = gates[0:4, 6:8, :], *(gate_row(i) for i in range(8, 14))
        R12 = gates[0:12, 14, :]
        prow = gates[:, 0:3, 0:P]
        lev_tmp = [gates[:, 15, i * P:(i + 1) * P] for i in range(2)]
        xs1 = gates[:, 16:24, :].rearrange("p a b -> p (a b)").rearrange("p (t d) -> p t d", t=NT)

        XHL = {"x": (xh, xl), "m1": (mh, ml), "m2": (m2h, m2l), "ym": (y2h, y2l), "y5": (y5h, y5l),
               "h0": (hh, hl), "h1": (hh, hl), "h2": (hh, hl)}
        for br in range(3):
            XHL[f"y{br}"] = (ybh[br], ybl[br])
        NORM = {"norm_mix": (x, xh, xl), "norm_xq": (x, xh, xl), "norm_ffn": (x, xh, xl), "norm_mem": (memx, mh, ml),
                "ffn1_pre_g_2": (x, xh, xl), "mix_pre_g_2": (x, xh, xl), "xa_pre_g_2": (x, xh, xl),
                "ffn2_pre_g_2": (x, xh, xl), "mem_g_2": (memx, m2h, m2l)}
        TO = {"fq": fq_, "fk": fk_, "sq": sq_, "sk": sk_, "mk": mk_, "mq": mq_, "qk": qk_, "xk": xk_, "xq": qk_,
              "pin": pin, "fv": fv_, "sv": sv_, "mv": mv_, "bv": bv_, "xv0": xv_[:, :, 0:512], "xv1": xv_[:, :, 512:1024]}

        def pcolumn(name, i=0):
            return pcol[:, COL[name] + i:COL[name] + i + 1]

        HN = {}
        for i in range(2):
            s = slice(2 * i, 2 * i + 2)
            HN[f"gq{i}"] = (gq_[:, s, :], gKb, gVb, 4, None, 1.0, float(HD) ** -0.5, None)
            HN[f"gk{i}"] = (gk_[:, s, :], gKb, gVb, 4, None, 1.0, 1.0, None)
            HN[f"go{i}"] = (gq_[:, s, :], gKb, gVb, 4, pcolumn("gdn_onorm"), 1.0 / HD, 1.0, gz_[:, s, :])
            HN[f"fq{i}"] = (fq_[:, s, :], S1, PT1, 6, gsc, 1.0 / HD, 1.0, None)
            HN[f"fk{i}"] = (fk_[:, s, :], S1, PT1, 6, pcolumn("fox_knorm"), 1.0 / HD, 1.0, None)
            HN[f"mq{i}"] = (mq_[:, s, :], S2[0], PT2[0], 4, pcolumn("mq_norm"), 1.0 / HD, 1.0, None)
            HN[f"mk{i}"] = (mk_[:, s, :], S2[0], PT2[0], 4, pcolumn("mk_norm"), 1.0 / HD, 1.0, None)

        HN_BEFORE = {}
        for jobs in (("gq0", "gk0", "gq1", "gk1", "go0", "go1"), ("fq0", "fq1", "fk0", "fk1"), ("mk0", "mk1", "mq0", "mq1")):
            HN_BEFORE |= dict(zip(jobs[1:], jobs))

        FACTOR = {"fox": 1.0, "mem": float(HD) ** -0.5, "moba": 64.0 ** -0.5, "xa": 256.0 ** -0.5}
        SLOPE = [2.0 ** (-(h + 1)) for h in range(8)]

        def lane(kind, h):
            l = 1 if kind == "fox" else h % 2
            s, pt = {"fox": (S1, PT1), "mem": (S2[l], PT2[l])}.get(kind, (S5[l], PT5[l]))
            return s, pt, 4 + 2 * l, 5 + 2 * l, nmx[l], rsm[l], rrc[l]

        def before(kind, h):
            d = 1 if kind == "fox" else 2
            return h - d if h >= d else None

        def values(kind, h):
            return {"fox": lambda: fv_[:, :, h * HD:(h + 1) * HD], "mem": lambda: mv_[:, :, h * HD:(h + 1) * HD],
                    "moba": lambda: bv_[:, :, h * 64:(h + 1) * 64], "xa": lambda: xv_[:, :, h * 256:(h + 1) * 256]}[kind]()

        def mat(t):
            return t[:, :].rearrange("p (a b) -> p a b", a=2) if len(t.shape) == 2 else t.rearrange("p h t -> p (h t)").rearrange("p (a b) -> p a b", a=2)

        def per_head(t):
            return t.rearrange("p (h e) -> p h e", h=NH)

        def flat(t):
            return t.rearrange("p a b -> p (a b)") if len(t.shape) == 3 else t

        block = fixed.enter_context(nc.Block())

        @block.sync
        def _(sp):
            sp.dma_start(x[:, :, :], w["x"].rearrange("(t p) d -> p t d", p=P)).then_inc(x_in, 16)
            sp.dma_start(prow, w["params"].rearrange("(j r) c -> r j c", r=P)).then_inc(par_in, 16)
            for c, ch in enumerate(chunks):
                if c == 1:
                    with nc.allow_non_contiguous_dma(reason="three numbers a head"):
                        sp.dma_start(per_gate, w["gate_params"]).then_inc(par_in, 16)
                if c >= RING:
                    sp.wait_ge(dve_done, at("lo", c - RING))
                for (a, b), src in ch["srcs"]:
                    dst = raw[c % RING][:, 0:src.shape[1] * width(ch)].rearrange("p (k n) -> p k n", n=width(ch))
                    sp.dma_start(dst[:, :, a:b], src).then_inc(raw_in[c % RING], 16)
            for t in range(NT):
                sp.wait_ge(dve_done, at("post2", len(chunks) - 1, t))
                sp.dma_start(out[t * P:(t + 1) * P, :], x[:, t, :]).then_inc(out_done, 16)
            sp.wait_ge(out_done, 16 * NT)

        @block.gpsimd
        def _(pool):
            linked = [0]

            def link(ins):
                linked[0] += 1
                ins.then_inc(pool_link, 1)
                pool.wait_ge(pool_link, linked[0])

            def select(outp, inp, pattern, base, cm, fill, op=ALU.is_ge):
                return pool.affine_select(out=outp, in_=inp, pattern=pattern, compare_op=op, fill=fill,
                                          base=base, channel_multiplier=cm)

            def consts():
                link(pool.memset(ident[:, :], 0.0))
                link(select(ident[:, :], ident[:, :], [[-1, P]], 0, 1, 1.0, ALU.not_equal))
                link(pool.memset(ones[:, :], 1.0))
                pool.memset(eps, EPS).then_inc(pool_done, 1)

            def consts2():
                link(pool.memset(sel[:, :, :], 0.0))
                link(select(sel[:, :, :], sel[:, :, :], [[-1, NH], [0, T]], 0, 1, 1.0, ALU.not_equal))
                link(pool.memset(cmask[:, :, :], 0.0))
                link(select(cmask[:, :, :], cmask[:, :, :], [[P, NT], [-1, T]], 0, 1, NEG))
                link(select(sbm[:, :], ones[:, :], [[1, P]], -1, -1, 0.0))
                link(pool.memset(sba[:, :], 0.0))
                link(select(sba[:, :], sba[:, :], [[1, P]], -1, -1, NEG))
                link(select(tri[:, :], ones[:, :], [[-1, P]], 0, 1, 0.0))
                link(pool.memset(gda[:, :], 0.0))
                link(select(gda[:, :], gda[:, :], [[-1, P]], 0, 1, NEG))
                link(select(gda[:, :], gda[:, :], [[CH, 2], [0, CH]], CH - 1, -1, NEG))
                link(pool.memset(gdat[:, :], 0.0))
                link(select(gdat[:, :], gdat[:, :], [[1, P]], 0, -1, NEG))
                link(select(gdat[:, :], gdat[:, :], [[-CH, 2], [0, CH]], 0, 1, NEG))
                link(select(strict[:, :], ones[:, :], [[-1, P]], -1, 1, 0.0))
                small_block = ident[:, :]
                for l in range(6):
                    s = 2 << l
                    big = lev_tmp[l % 2]
                    link(select(big, ones[:, :], [[-s, P // s], [0, s]], 0, 1, 0.0))
                    link(select(big, big, [[s, P // s], [0, s]], s - 1, -1, 0.0))
                    ins = pool.tensor_tensor(lev[:, l, :], big, small_block, ALU.subtract)
                    if l < 5:
                        link(ins)
                    small_block = big
                ins.then_inc(pool_done, 1)

            def g_eye(t):
                if t:
                    pool.wait_ge(dve_done, at("r_s", 0, 1))
                    pool.wait_ge(pe_done, at("g_uw", 0))
                eye = ident[:, :].unsqueeze(1).to_broadcast([P, NH, P])
                pool.tensor_copy(gX[:, :, :], eye)
                pool.tensor_copy(gY[:, :, :], eye).then_inc(pool_done, 1)

            def l_mask(t, l):
                pool.wait_ge(dve_done, at("g_m", t))
                if l >= 2:
                    pool.wait_ge(pe_done, at("l_u", t, l - 2))
                    if l == 2:
                        pool.wait_ge(dve_done, at("l_upd", t, 0))
                elif t:
                    pool.wait_ge(dve_done, at("r_s", 0, 1))
                pool.tensor_tensor(gMs[l % 2][:, :, :], gM[:, :, :], lev[:, l, :].unsqueeze(1).to_broadcast([P, NH, P]),
                                   ALU.mult).then_inc(pool_done, 1)

            def mem_load():
                pool.wait_ge(dve_done, at("mixl", 3))
                pool.dma_start(memx[:, :, :], w["mem"].rearrange("(t p) d -> p t d", p=P)).then_inc(mem_in, 16)
                pool.memset(small[:, 60:61], 0.0).then_inc(pool_done, 1)

            def gain_load(i):
                if i:
                    pool.wait_ge(dve_done, at("post2", POSTS[i - 1], 1))
                else:
                    pool.wait_ge(dve_done, at("nl", "norm_ffn", 3))
                name = ("ffn1_post_g_2", "mix_post_g_2", "xa_post_g_2", "ffn2_post_g_2")[i]
                pool.dma_start(gain[:, :], w[name].to_broadcast([P, D])).then_inc(gains_in, 16)
                pool.memset(small[:, 61:62], 0.0).then_inc(pool_done, 1)

            def mem2_load():
                pool.wait_ge(dve_done, at("nd", "norm_mem", 1))
                pool.dma_start(memx[:, :, :], w["mem_2"].rearrange("(t p) d -> p t d", p=P)).then_inc(mem2_in, 16)
                pool.memset(small[:, 62:63], 0.0).then_inc(pool_done, 1)

            def pool_tables():
                pool.wait_ge(dve_done, at("nl", "mix_pre_g_2", 3))
                pool.dma_start(poolw[:, :, :], w["pool_w_2"].rearrange("(g c) d -> c g d", c=P)).then_inc(pw_in, 16)
                link(pool.iota(dist[:, :, :], [[P, NT], [-1, T]], 0, 1, allow_small_or_imprecise_dtypes=True))
                link(select(dist[:, :, :], dist[:, :, :], [[P, NT], [-1, T]], 0, 1, -NEG))
                link(pool.iota(rcnt[:, :, 0:16], [[0, 4], [1, 16]], 1, 0, allow_small_or_imprecise_dtypes=True))
                for g in range(4):
                    pool.memset(rcnt[:, g, 16:T], 1.0 / (2 << g))
                    ins = pool.tensor_scalar(rcnt[:, g, 0:16], rcnt[:, g, 0:16], float(2 << g), None, ALU.min)
                ins.then_inc(pool_done, 1)

            run(pool, "pool", locals())

        @block.tensor
        def _(pe):
            def params():
                pe.wait_ge(par_in, 16 * N_PAR)
                pe.wait_ge(pool_done, at("consts"))
                for j in range(3):
                    ins = pe.transpose(bank(4)[:, j * P:(j + 1) * P], prow[:, j, :], ident[:, :])
                ins.then_inc(pe_done, 1)

            def mm(c, part):
                ch = chunks[c]
                slot, (Xh, Xl), b = c % RING, XHL[ch["x"]], ch["banks"]
                if part == 0:
                    pe.wait_ge(dve_done, at("lo", c))
                    for step in plan.ready[c]:
                        pe.wait_ge(DONE[plan.engine[step[0]]], at(*step))
                    for step in plan.bank_wait.get(("mm", c, 0), []):
                        pe.wait_ge(DONE[plan.engine[step[0]]], at(*step))
                n = width(ch)
                wh, wl = (t[slot][:, :].rearrange("p (k n) -> p k n", n=n) for t in (whi, wlo))
                if ch["kind"] in "SA":
                    if ch["kind"] == "S":
                        cols_, o = slice(0, P), bank(b[0])[:, 0:T]
                        ks = range(4 * part, 4 * part + 4)
                    else:
                        cols_, o = slice(part * P, (part + 1) * P), bank(b[0])[:, part * T:(part + 1) * T]
                        ks = range(KD)
                    for k in ks:
                        if k % 2 == 0 and part == 0 and c in plan.fresh and plan.fresh[c]:
                            pe.wait_ge(dve_done, at(*plan.fresh[c], k // 2))
                        for i, (a, v) in enumerate(((wh, Xh), (wh, Xl), (wl, Xh))):
                            ins = pe.matmul(o, a[:, k, cols_], v[:, k, :],
                                            start=(k == 0 and i == 0), stop=(k == KD - 1 and i == 2))
                elif ch["kind"] == "O":
                    for m in range(2):
                        o = (2 * part + m) * P
                        for k in range(NH):
                            for i, (a, v) in enumerate(((wh, Xh), (wh, Xl), (wl, Xh))):
                                ins = pe.matmul(bank(b[part])[:, m * T:(m + 1) * T], a[:, k, o:o + P], v[:, k, :],
                                                start=(k == 0 and i == 0), stop=(k == NH - 1 and i == 2))
                elif ch["kind"] == "V":
                    for kk in range(2 * part, 2 * part + 2):
                        k = 4 * ch["half"] + kk
                        if k % 2 == 0 and c in plan.fresh and plan.fresh[c]:
                            pe.wait_ge(dve_done, at(*plan.fresh[c], k // 2))
                        for t in range(NT):
                            for i, (v, a) in enumerate(((Xh, wh), (Xh, wl), (Xl, wh))):
                                ins = pe.matmul(bank(b[t]), v[:, k, t * P:(t + 1) * P], a[:, kk, :],
                                                start=(k == 0 and i == 0), stop=(k == KD - 1 and i == 2))
                else:
                    k = 2 * ch["j"] + part
                    if ch["name"] == "w_out" and part == 0:
                        pe.wait_ge(dve_done, at("mixl", ch["j"]))
                    for t in range(NT):
                        for nb in range(2):
                            for i, (v, a) in enumerate(((Xh, wh), (Xh, wl), (Xl, wh))):
                                ins = pe.matmul(bank(b[2 * t + nb]), v[:, k, t * P:(t + 1) * P], a[:, part, nb * 512:(nb + 1) * 512],
                                                start=(k == 0 and i == 0), stop=(ch["last"] and part == 1 and i == 2))
                ins.then_inc(pe_done, 1)

            def nt(name, j):
                src = xs1 if name == "norm_mix" else xs
                pe.wait_ge(dve_done, at("nd", name, 1))
                for step in plan.bank_wait[("nt", name, j)]:
                    pe.wait_ge(DONE[plan.engine[step[0]]], at(*step))
                for k in range(2):
                    for t in range(NT):
                        kt = 2 * j + k
                        ins = pe.transpose(bank(j)[:, k * T + t * P:k * T + (t + 1) * P], src[:, t, kt * P:(kt + 1) * P], ident[:, :])
                ins.then_inc(pe_done, 1)

            def rows0p():
                pe.wait_ge(dve_done, at("rows0"))
                for i in range(3):
                    ins = pe.matmul(bank(4 + i // 2)[0:4, (i % 2) * T:(i % 2 + 1) * T], ident[0:12, 4 * i:4 * i + 4], R12,
                                    start=True, stop=True)
                ins.then_inc(pe_done, 1)

            def rows6():
                pe.wait_ge(dve_done, at("rows5"))
                pe.wait_ge(dve_done, at("params_c"))
                for t in range(NT):
                    for j, row in enumerate((BETA, BEGC, ETAIL)):
                        o = (t * 3 + j) * 4
                        ins = pe.transpose(bank(4)[:, o:o + 4], row[:, t * P:(t + 1) * P], ident[0:4, 0:4])
                ins.then_inc(pe_done, 1)

            def hn_sum(job):
                dst, sq, rr, b, *_ = HN[job]
                pe.wait_ge(act_done, at("hn_sq", job))
                if job == "gq0":
                    pe.wait_ge(dve_done, at("rows7"))
                if job == "go0":
                    pe.wait_ge(dve_done, at("r_s", 1, 1))
                elif job in HN_BEFORE:
                    pe.wait_ge(dve_done, at("hn_mul", HN_BEFORE[job]))
                pe.matmul(bank(b), ones[:, :], flat(sq[:]), start=True, stop=True).then_inc(pe_done, 1)

            def g_dec(t):
                pe.wait_ge(dve_done, at("hn_mul", "gk1"))
                pe.wait_ge(pool_done, at("consts2"))
                if t:
                    pe.wait_ge(act_done, at("r_oc", 0, 1))
                    pe.wait_ge(dve_done, at("r_s", 0, 1))
                s = slice(t * P, (t + 1) * P)
                for h in range(NH):
                    e = slice(h * P, (h + 1) * P)
                    pe.matmul(bank(4)[:, e], gc[0:4, s], sel[0:4, h, 0:P], start=True, stop=False)
                    pe.matmul(bank(4)[:, e], sel[0:4, h, 0:P], ngc[0:4, s], start=False, stop=True)
                for h in range(NH):
                    e = slice(h * P, (h + 1) * P)
                    pe.matmul(bank(5)[:, e], sel[0:4, h, 0:P], gc[0:4, s], start=True, stop=False)
                    ins = pe.matmul(bank(5)[:, e], ngc[0:4, s], sel[0:4, h, 0:P], start=False, stop=True)
                ins.then_inc(pe_done, 1)

            def g_kk(t):
                pe.wait_ge(dve_done, at("g_mask", t))
                s = slice(t * P, (t + 1) * P)
                for h in range(NH):
                    pe.matmul(bank(4)[:, h * P:(h + 1) * P], gk_[:, h, s], gk_[:, h, s], start=True, stop=True)
                for h in range(NH):
                    ins = pe.matmul(bank(5)[:, h * P:(h + 1) * P], gk_[:, h, s], gq_[:, h, s], start=True, stop=True)
                ins.then_inc(pe_done, 1)

            def g_turn(t):
                pe.wait_ge(dve_done, at("g_m", t))
                s = slice(t * P, (t + 1) * P)
                for b, src in ((4, gk_), (5, gv_)):
                    for h in range(NH):
                        ins = pe.transpose(bank(b)[:, h * P:(h + 1) * P], src[:, h, s], ident[:, :])
                ins.then_inc(pe_done, 1)

            def l_u(t, l):
                pe.wait_ge(pool_done, at("l_mask", t, l))
                if l:
                    pe.wait_ge(dve_done, at("l_upd", t, l - 1))
                else:
                    pe.wait_ge(act_done, at("g_kb", t))
                    pe.wait_ge(dve_done, at("g_vb", t))
                for h in range(NH):
                    o = bank(4)[:, h * P:(h + 1) * P]
                    if l == 0:
                        ins = pe.transpose(o, gMs[0][:, h, :], ident[:, :])
                    else:
                        ins = pe.matmul(o, gMs[l % 2][:, h, :], gY[:, h, :], start=True, stop=True)
                ins.then_inc(pe_done, 1)

            def l_x(t, l):
                pe.wait_ge(act_done, at("l_uc", t, l))
                if l < 5:
                    for h in range(NH):
                        pe.matmul(bank(5)[:, h * P:(h + 1) * P], gU[:, h, :], gX[:, h, :], start=True, stop=True)
                for h in range(NH):
                    ins = pe.matmul(bank(4)[:, h * P:(h + 1) * P], gX[:, h, :], gU[:, h, :], start=True, stop=True)
                ins.then_inc(pe_done, 1)

            def g_uw(t):
                pe.wait_ge(dve_done, at("l_upd", t, 5))
                for h in range(NH):
                    pe.matmul(bank(4)[:, h * P:(h + 1) * P], gY[:, h, :], gVb[:, h, :], start=True, stop=True)
                for h in range(NH):
                    ins = pe.matmul(bank(5)[:, h * P:(h + 1) * P], gKb[:, h, :], gY[:, h, :], start=True, stop=True)
                ins.then_inc(pe_done, 1)

            def g_bc(t):
                pe.wait_ge(dve_done, at("g_u", t))
                for h in range(NH):
                    ins = pe.matmul(bank(4)[:, h * P:(h + 1) * P], sel[0:4, h, 0:P], gc[0:4, t * P:(t + 1) * P], start=True, stop=True)
                ins.then_inc(pe_done, 1)

            def r_ws(t, j):
                r = slice(j * CH, (j + 1) * CH)
                pe.wait_ge(act_done, at("g_w", t))
                pe.wait_ge(dve_done, at("g_qg", t))
                if j:
                    pe.wait_ge(dve_done, at("r_s", t, 0))
                for h in range(NH):
                    ins = pe.matmul(bank(4)[r, h * P:(h + 1) * P], gU[:, h, r], gS[:, h, :], start=True, stop=True)
                ins.then_inc(pe_done, 1)

            def r_o(t, j):
                r = slice(j * CH, (j + 1) * CH)
                s = slice(t * P + j * CH, t * P + (j + 1) * CH)
                pe.wait_ge(dve_done, at("r_vn", t, j))
                if j:
                    pe.wait_ge(act_done, at("r_oc", t, 0))
                for h in range(NH):
                    o = bank(5)[:, h * CH:(h + 1) * CH]
                    pe.matmul(o, gS[:, h, :], gq_[:, h, s], start=True, stop=False)
                    pe.matmul(o, gMs0[r, h, :], gAT[r, h, r], start=False, stop=True)
                for h in range(NH):
                    ins = pe.matmul(bank(4)[:, h * P:(h + 1) * P], gKt[r, h, :], gMs0[r, h, :], start=True, stop=True)
                ins.then_inc(pe_done, 1)

            def sc(kind, h):
                s_, pt_, b, *_ = lane(kind, h)
                p = before(kind, h)
                if p is not None:
                    pe.wait_ge(act_done, at("oc", kind, p))
                    if kind != "fox":
                        pe.wait_ge(dve_done, at("ol", kind, p))
                if kind == "fox":
                    pe.wait_ge(dve_done, at("hn_mul", "fk1"))
                    pe.wait_ge(pool_done, at("consts2"))
                elif kind == "mem":
                    pe.wait_ge(dve_done, at("hn_mul", "mq1"))
                elif kind == "moba":
                    pe.wait_ge(act_done, at("copy", chunk_of("qk", 2 + h // 4)))
                else:
                    pe.wait_ge(act_done, at("copy", chunk_of("xq", h)))
                for t in range(NT):
                    q = slice(t * P, (t + 1) * P)
                    o = bank(b)[:, t * T:(t + 1) * T]
                    if kind == "fox":
                        pe.matmul(o, fq_[:, h, q], fk_[:, h, :], start=True, stop=False)
                        pe.matmul(o, cf[0:4, q], sel[0:4, h, :], start=False, stop=False)
                        ins = pe.matmul(o, sel[0:4, h, 0:P], ncf[0:4, :], start=False, stop=True)
                    elif kind == "mem":
                        ins = pe.matmul(o, mq_[:, h, q], mk_[:, h, :], start=True, stop=True)
                    elif kind == "moba":
                        r = slice(64 * (h % 2), 64 * (h % 2) + 64)
                        ins = pe.matmul(o, qk_[r, h // 2, q], qk_[r, 4 + h // 2, :], start=True, stop=True)
                    else:
                        for k in range(2):
                            ins = pe.matmul(o, qk_[:, 2 * h + k, q], xk_[:, 2 * h + k, :], start=(k == 0), stop=(k == 1))
                ins.then_inc(pe_done, 1)

            def pt(kind, h):
                s_, pt_, b0, b, *_ = lane(kind, h)
                pe.wait_ge(dve_done, at("pn", kind, h))
                p = before(kind, h)
                if p is not None:
                    pe.wait_ge(act_done, at("pc", kind, p))
                for kb in range(2):
                    for t in range(NT):
                        ins = pe.transpose(bank(b)[:, kb * T + t * P:kb * T + (t + 1) * P],
                                           s_[:, t * T + kb * P:t * T + (kb + 1) * P], ident[:, :])
                ins.then_inc(pe_done, 1)

            def pv(kind, h):
                s_, pt_, b, *_ = lane(kind, h)
                pe.wait_ge(act_done, at("pc", kind, h))
                if kind in ("mem", "xa", "moba", "fox"):
                    pe.wait_ge(act_done, at("copy", chunk_of({"mem": "mv", "xa": "xv1", "moba": "bv", "fox": "fv"}[kind], None)))
                v = values(kind, h)
                r0 = 64 * (h % 2) if kind == "moba" else 0
                for m in range(2 if kind == "xa" else 1):
                    width_ = 64 if kind == "moba" else P
                    o = bank(b)[r0:r0 + width_, m * T:(m + 1) * T]
                    for kb in range(2):
                        ins = pe.matmul(o, v[:, kb, m * P:m * P + width_], pt_[:, kb * T:(kb + 1) * T], start=(kb == 0), stop=(kb == 1))
                ins.then_inc(pe_done, 1)

            def z_s(h):
                if h:
                    pe.wait_ge(act_done, at("z_oc", h - 1))
                else:
                    pe.wait_ge(act_done, at("oc", "fox", NH - 1))
                    pe.wait_ge(act_done, at("copy", chunk_of("sk", 1)))
                pe.matmul(bank(6)[:, 0:T], sk_[:, h, 0:P], sq_[:, h, :], start=True, stop=True)
                pe.matmul(bank(6)[:, T:T + P], sk_[:, h, P:T], sq_[:, h, P:T], start=True, stop=True).then_inc(pe_done, 1)

            def z_rc(h):
                pe.wait_ge(dve_done, at("z_lk", h))
                if h:
                    pe.wait_ge(dve_done, at("z_w", h - 1))
                pe.matmul(bank(7)[:, T:T + P], tri[:, :], PT1[:, T:T + P], start=True, stop=True)
                pe.matmul(bank(7)[:, 0:T], tri[:, :], PT1[:, 0:T], start=True, stop=False)
                pe.matmul(bank(7)[:, P:T], ones[:, :], PT1[:, T:T + P], start=False, stop=True).then_inc(pe_done, 1)

            def z_o(h):
                pe.wait_ge(act_done, at("z_x", h))
                pe.wait_ge(act_done, at("copy", chunk_of("sv", None)))
                pe.matmul(bank(6)[:, 0:T], sv_[:, 0, h * HD:(h + 1) * HD], S1[:, 0:T], start=True, stop=False)
                pe.matmul(bank(6)[:, P:T], sv_[:, 1, h * HD:(h + 1) * HD], S1[:, T:T + P], start=False, stop=True).then_inc(pe_done, 1)

            def pl_mm(g):
                pe.wait_ge(dve_done, at("pl_win", g))
                if g == 0:
                    pe.wait_ge(pw_in, 16)
                    pe.wait_ge(dve_done, at("ol", "moba", 6))
                    pe.wait_ge(dve_done, at("ol", "moba", 7))
                pe.matmul(bank(4 + g)[:, 0:T], poolw[:, g, :], pin[:, g, :], start=True, stop=True).then_inc(pe_done, 1)

            run(pe, "pe", locals())

        @block.scalar
        def _(act):
            linked = [0]

            def link(ins):
                linked[0] += 1
                ins.then_inc(act_link, 1)
                act.wait_ge(act_link, linked[0])

            nc.scalar.preload_act_table_set(LOG_EXP)

            def tables(phase):
                nc.scalar.preload_act_table_set(LOG_EXP)
                act.activation(small[:, 59:60], eps, ACT.Copy).then_inc(act_done, 1)

            def hi(c):
                act.wait_ge(raw_in[c % RING], landed[c])
                if c >= RING:
                    act.wait_ge(pe_done, at("mm", c - RING, 1))
                act.activation(whi[c % RING][:, :], raw[c % RING][:, :], ACT.Copy).then_inc(act_done, 1)

            def ns(name, t):
                src, junk = NORM[name][0], (xs1 if name == "norm_mix" else xs)
                if name == "norm_mix":
                    act.wait_ge(x_in, 16)
                elif name == "norm_mem":
                    act.wait_ge(mem_in, 16)
                elif name == "mem_g_2":
                    act.wait_ge(mem2_in, 16)
                if name in ("norm_xq", "norm_ffn", "ffn1_pre_g_2"):
                    act.wait_ge(dve_done, at("resid", LAST_ROWS[name], t))
                elif name in LAST_ROWS:
                    act.wait_ge(dve_done, at("post2", LAST_ROWS[name], t))
                if name in NORM_BEFORE:
                    act.wait_ge(pe_done, at("nt", NORM_BEFORE[name], 3))
                act.activation(junk[:, t, :], src[:, t, :], ACT.Square, accum_out=ms[:, t:t + 1]).then_inc(act_done, 1)

            def nr(name):
                act.wait_ge(pool_done, at("consts"))
                link(act.activation(rn, ms, ACT.Ln, bias=eps, scale=1.0 / D))
                act.activation(rn, rn, ACT.Exp, scale=-0.5).then_inc(act_done, 1)

            def nh(name, j):
                act.wait_ge(pe_done, at("nt", name, j))
                act.wait_ge(dve_done, at("params_c"))
                gname = name
                for k in range(2):
                    kt = 2 * j + k
                    ins = act.activation(NORM[name][1][:, kt, :], bank(j)[:, k * T:(k + 1) * T], ACT.Copy, scale=pcolumn(gname, kt))
                ins.then_inc(act_done, 1)

            def rows2():
                act.wait_ge(dve_done, at("rows1"))
                act.activation(ealog, alog, ACT.Exp)
                act.activation(EBR, GBR, ACT.Exp, scale=-1.0)
                link(act.activation(E2, W2, ACT.Abs))
                link(act.activation(E2, E2, ACT.Exp, scale=-1.0))
                act.activation(E2, E2, ACT.Ln, bias=1.0).then_inc(act_done, 1)

            def rows4():
                act.wait_ge(dve_done, at("rows3"))
                act.activation(EGC, gc[:, :], ACT.Exp)
                act.activation(ETAIL, TAIL, ACT.Exp).then_inc(act_done, 1)

            def cv_mul(c):
                i = chunks[c]["i"]
                act.wait_ge(pe_done, at("mm", c, 1))
                dst = (gq_, gk_, gv_)[i // 2]
                for m in range(2):
                    ins = act.activation(dst[:, 2 * (i % 2) + m, :], bank(chunks[c]["banks"][0])[:, m * T:(m + 1) * T], ACT.Copy,
                                         scale=pcolumn("gdn_conv", 3 * 12 + 2 * i + m))
                ins.then_inc(act_done, 1)

            def cv_silu(c):
                i = chunks[c]["i"]
                act.wait_ge(dve_done, at("cv_add", c))
                d = (gq_, gk_, gv_)[i // 2][:, 2 * (i % 2):2 * (i % 2) + 2, :]
                act.activation(d, d, ACT.Silu).then_inc(act_done, 1)

            def copy(c):
                ch = chunks[c]
                act.wait_ge(pe_done, at("mm", c, 1))
                if ch["kind"] == "V":
                    for t in range(NT):
                        ins = act.activation(TO[ch["to"]][:, t, :], bank(ch["banks"][t]), ACT.Copy)
                elif ch["evac"] == "copy":
                    ins = act.activation(TO[ch["to"]][:, 2 * ch["i"]:2 * ch["i"] + 2, :],
                                         bank(ch["banks"][0]).rearrange("p (a b) -> p a b", a=2), ACT.Copy)
                elif ch["evac"] == "gz":
                    ins = act.activation(gz_[:, 2 * ch["i"]:2 * ch["i"] + 2, :],
                                         bank(ch["banks"][0]).rearrange("p (a b) -> p a b", a=2), ACT.Copy)
                else:
                    if ch["i"] == 0:
                        act.wait_ge(dve_done, at("rows7"))
                        act.wait_ge(pool_done, at("consts2"))
                    for m in range(2):
                        f = 2 * ch["i"] + m
                        ins = act.activation(gates[:, f, :], bank(ch["banks"][0])[:, m * T:(m + 1) * T], ACT.Identity,
                                             bias=pcolumn("gate_bias", f))
                ins.then_inc(act_done, 1)

            def gzs():
                act.activation(gz_[:, :, :], gz_[:, :, :], ACT.Silu)
                nc.scalar.preload_act_table_set(LOG_EXP)
                act.activation(small[:, 59:60], eps, ACT.Copy).then_inc(act_done, 1)

            def gsig(br):
                g = gates[:, 8 * br:8 * br + 8, :]
                act.activation(g, g, ACT.Sigmoid).then_inc(act_done, 1)

            def hn_sq(job):
                dst, sq, rr, b, *_ = HN[job]
                act.activation(mat(sq), dst, ACT.Square).then_inc(act_done, 1)

            def hn_r(job):
                dst, sq, rr, b, g, inv, f, gate = HN[job]
                act.wait_ge(pe_done, at("hn_sum", job))
                if job in HN_BEFORE:
                    act.wait_ge(dve_done, at("hn_mul", HN_BEFORE[job]))
                link(act.activation(flat(rr[:]), bank(b), ACT.Ln, bias=eps, scale=inv))
                act.activation(flat(rr[:]), flat(rr[:]), ACT.Exp, scale=-0.5).then_inc(act_done, 1)

            def g_exp(t):
                act.wait_ge(dve_done, at("g_mask", t))
                act.activation(gM[:, :, :], gM[:, :, :], ACT.Exp)
                act.activation(gAT[:, :, :], gAT[:, :, :], ACT.Exp).then_inc(act_done, 1)

            def g_kb(t):
                act.wait_ge(pe_done, at("g_turn", t))
                act.wait_ge(dve_done, at("rows7"))
                for h in range(NH):
                    act.activation(gKb[:, h, :], bank(4)[:, h * P:(h + 1) * P], ACT.Copy, scale=gcols[:, t, 1, h:h + 1])
                    ins = act.activation(gKt[:, h, :], bank(4)[:, h * P:(h + 1) * P], ACT.Copy, scale=gcols[:, t, 2, h:h + 1])
                ins.then_inc(act_done, 1)

            def l_uc(t, l):
                act.wait_ge(pe_done, at("l_u", t, l))
                act.activation(gU[:, :, :], per_head(bank(4)), ACT.Copy).then_inc(act_done, 1)

            def g_w(t):
                act.wait_ge(pe_done, at("g_uw", t))
                act.activation(gU[:, :, :], per_head(bank(5)), ACT.Copy).then_inc(act_done, 1)

            def g_egc(t):
                act.wait_ge(pe_done, at("g_bc", t))
                act.activation(gX[:, :, :], per_head(bank(4)), ACT.Exp).then_inc(act_done, 1)

            def r_oc(t, j):
                act.wait_ge(pe_done, at("r_o", t, j))
                s = slice(t * P + j * CH, t * P + (j + 1) * CH)
                act.activation(gq_[:, :, s], bank(5)[:, 0:NH * CH].rearrange("p (h e) -> p h e", h=NH), ACT.Copy).then_inc(act_done, 1)

            def ex(kind, h):
                s_, pt_, b, b2, nm, rs, rc = lane(kind, h)
                act.wait_ge(dve_done, at("sm", kind, h))
                f = FACTOR[kind]
                if before(kind, h) is not None:
                    act.wait_ge(pe_done, at("pt", kind, before(kind, h)))
                src = s_ if kind in ("fox", "moba") else bank(b)
                for t in range(NT):
                    ins = act.activation(s_[:, t * T:(t + 1) * T], src[:, t * T:(t + 1) * T], ACT.Exp, bias=nm[:, t:t + 1],
                                         scale=f, accum_out=rs[:, t:t + 1])
                ins.then_inc(act_done, 1)

            def pc(kind, h):
                s_, pt_, b0, b, *_ = lane(kind, h)
                act.wait_ge(pe_done, at("pt", kind, h))
                if before(kind, h) is not None:
                    act.wait_ge(pe_done, at("pv", kind, before(kind, h)))
                act.activation(pt_[:, :], bank(b), ACT.Copy).then_inc(act_done, 1)

            def oc(kind, h):
                s_, pt_, b, *_ = lane(kind, h)
                act.wait_ge(pe_done, at("pv", kind, h))
                if kind == "fox":
                    ins = act.activation(fq_[:, h, :], bank(b)[:, 0:T], ACT.Copy)
                elif kind == "mem":
                    ins = act.activation(y2h[:, h, :], bank(b)[:, 0:T], ACT.Copy)
                elif kind == "moba":
                    r = slice(64 * (h % 2), 64 * (h % 2) + 64)
                    ins = act.activation(y5h[r, h // 2, :], bank(b)[r, 0:T], ACT.Copy)
                else:
                    ins = act.activation(y5h[:, 2 * h:2 * h + 2, :], bank(b).rearrange("p (a b) -> p a b", a=2), ACT.Copy)
                ins.then_inc(act_done, 1)

            def z_e(h):
                act.wait_ge(pe_done, at("z_s", h))
                if h:
                    act.wait_ge(pe_done, at("z_o", h - 1))
                else:
                    act.wait_ge(pe_done, at("pv", "fox", NH - 1))
                f = float(HD) ** -0.5
                n = T + P
                act.activation(S1[:, 0:n], bank(6)[:, 0:n], ACT.Copy, scale=f)
                link(act.activation(PT1[:, 0:n], bank(6)[:, 0:n], ACT.Abs, scale=f))
                link(act.activation(PT1[:, 0:n], PT1[:, 0:n], ACT.Exp, scale=-1.0))
                act.activation(PT1[:, 0:n], PT1[:, 0:n], ACT.Ln, bias=1.0).then_inc(act_done, 1)

            def z_x(h):
                act.wait_ge(dve_done, at("z_w", h))
                act.activation(S1[:, 0:T + P], S1[:, 0:T + P], ACT.Exp).then_inc(act_done, 1)

            def z_oc(h):
                act.wait_ge(pe_done, at("z_o", h))
                act.activation(sq_[:, h, :], bank(6)[:, 0:T], ACT.Copy).then_inc(act_done, 1)

            def yh(br):
                act.wait_ge(pe_done, at("z_o", NH - 1))
                act.wait_ge(dve_done, at("hn_mul", "fk1"))
                if br == 1:
                    act.wait_ge(dve_done, at("hn_mul", "go1"))
                act.activation(ybh[br][:, :, :], (fq_, gq_, sq_)[br][:, :, :], ACT.Copy).then_inc(act_done, 1)

            def mixh(q):
                act.wait_ge(dve_done, at("mix", q))
                act.activation(xh[:, 2 * q:2 * q + 2, :], gates[:, 2 * q:2 * q + 2, :], ACT.Copy).then_inc(act_done, 1)

            def ca(i):
                cg, cu = pair(0, i)
                act.wait_ge(pe_done, at("mm", cu, 1))
                if i >= 2:
                    act.wait_ge(dve_done, at("fm", 0, i - 2))
                for a, c in enumerate((cg, cu)):
                    for m in range(2):
                        f = a * KF + 2 * i + m
                        ins = act.activation(CA[i % 2][:, a, m * T:(m + 1) * T], bank(chunks[c]["banks"][0])[:, m * T:(m + 1) * T],
                                             ACT.Identity, scale=pcolumn("ffn_conv", 2 * 2 * KF + f), bias=pcolumn("ffn_conv_b", f))
                ins.then_inc(act_done, 1)

            def fs(f, i):
                cg, cu = pair(f, i)
                if i >= 2:
                    act.wait_ge(dve_done, at("fl", f, i - 2))
                if f == 0:
                    act.wait_ge(dve_done, at("cd", i))
                    ins = act.activation(SG[i % 2][:, :], CA[i % 2][:, 0, :], ACT.Silu)
                else:
                    act.wait_ge(pe_done, at("mm", cg, 1))
                    ins = act.activation(SG[i % 2][:, :], bank(chunks[cg]["banks"][0]), ACT.Silu)
                ins.then_inc(act_done, 1)

            def fh(f, i):
                act.wait_ge(dve_done, at("fm", f, i))
                act.activation(hh[:, 2 * i:2 * i + 2, :], mat(SG[i % 2]), ACT.Copy).then_inc(act_done, 1)

            def post1(c, t):
                act.wait_ge(pe_done, at("mm", c, 1))
                if t:
                    act.wait_ge(dve_done, at("post0", c, 1))
                junk = XHL[chunks[c]["x"]][0][:, 4 * t:4 * t + 4, :].rearrange("p a b -> p (a b)")
                act.activation(junk, banks[:, 4 + 2 * t:6 + 2 * t, :].rearrange("p a b -> p (a b)"), ACT.Square,
                               accum_out=ms[:, t:t + 1]).then_inc(act_done, 1)

            def post_r(c):
                link(act.activation(rn, ms, ACT.Ln, bias=eps, scale=1.0 / D))
                act.activation(rn, rn, ACT.Exp, scale=-0.5).then_inc(act_done, 1)

            def pl_h(g):
                act.wait_ge(pe_done, at("pl_mm", g))
                act.activation(y5h[:, 4 + g, :], bank(4 + g)[:, 0:T], ACT.Copy, scale=pcolumn("pool_scale_2", g)).then_inc(act_done, 1)

            run(act, "act", locals())

        @block.vector
        def _(dve):
            linked = [0]

            def link(ins):
                linked[0] += 1
                ins.then_inc(dve_link, 1)
                dve.wait_ge(dve_link, linked[0])

            def lo(c):
                dve.wait_ge(act_done, at("hi", c))
                dve.tensor_tensor(wlo[c % RING][:, :], raw[c % RING][:, :], whi[c % RING][:, :], ALU.subtract).then_inc(dve_done, 1)

            def params_c():
                dve.wait_ge(pe_done, at("params"))
                link(dve.tensor_copy(pcol[:, :], bank(4)[:, 0:3 * P]))
                dve.tensor_scalar(gsc, pcolumn("fox_qnorm"), float(HD) ** -0.5, None, ALU.mult).then_inc(dve_done, 1)

            def nd(name, t):
                dst = xs1 if name == "norm_mix" else xs
                dve.wait_ge(act_done, at("nr", name))
                dve.tensor_scalar(dst[:, t, :], NORM[name][0][:, t, :], rn[:, t:t + 1], None, ALU.mult).then_inc(dve_done, 1)

            def nl(name, j):
                dve.wait_ge(act_done, at("nh", name, j))
                _, h_, l_ = NORM[name]
                for k in range(2):
                    kt = 2 * j + k
                    ins = dve.scalar_tensor_tensor(l_[:, kt, :], bank(j)[:, k * T:(k + 1) * T], pcolumn(name, kt), h_[:, kt, :],
                                                   ALU.mult, ALU.subtract)
                ins.then_inc(dve_done, 1)

            def rows0():
                dve.wait_ge(pe_done, at("mm", chunk_of("rows", None), 1))
                dve.tensor_copy(R12, bank(chunks[chunk_of("rows", None)]["banks"][0])[0:12, 0:T]).then_inc(dve_done, 1)

            def rows1():
                dve.wait_ge(pe_done, at("rows0p"))
                dve.wait_ge(par_in, 16 * N_PAR)
                dve.tensor_copy(GBR, bank(4)[0:4, 0:T])
                dve.tensor_scalar(W2[:, 1, :], bank(4)[0:4, T:2 * T], dtb, None, ALU.add)
                dve.tensor_scalar(W2[:, 0, :], bank(5)[0:4, 0:T], fbias, -1.0, ALU.add, ALU.mult).then_inc(dve_done, 1)

            def rows3():
                dve.wait_ge(act_done, at("rows2"))
                link(dve.tensor_scalar(EBR, EBR, 1.0, None, ALU.add))
                dve.reciprocal(BETA, EBR)
                link(dve.scalar_tensor_tensor(SP2, W2, 0.0, E2, ALU.max, ALU.add))
                dve.tensor_scalar(SP2[:, 0, :], SP2[:, 0, :], -1.0, None, ALU.mult)
                link(dve.tensor_scalar(GLOG, SP2[:, 1, :], ealog, -1.0, ALU.mult, ALU.mult))
                one = ones[0:4, 0:1]
                dve.tensor_tensor_scan(cf[:, :], one.to_broadcast([4, T]), SP2[:, 0, :], 0.0, ALU.mult, ALU.add)
                for j in range(T // CH):
                    s = slice(j * CH, (j + 1) * CH)
                    ins = dve.tensor_tensor_scan(gc[:, s], one.to_broadcast([4, CH]), GLOG[:, s], 0.0, ALU.mult, ALU.add)
                link(ins)
                dve.tensor_scalar(ncf[:, :], cf[:, :], -1.0, None, ALU.mult)
                dve.tensor_scalar(ngc[:, :], gc[:, :], -1.0, None, ALU.mult)
                gcv = gc[:, :].rearrange("h (j c) -> h j c", c=CH)
                dve.tensor_tensor(TAIL.rearrange("h (j c) -> h j c", c=CH), gcv[:, :, CH - 1:CH].to_broadcast([4, T // CH, CH]), gcv,
                                  ALU.subtract).then_inc(dve_done, 1)

            def rows5():
                dve.wait_ge(act_done, at("rows4"))
                dve.tensor_tensor(BEGC, BETA, EGC, ALU.mult).then_inc(dve_done, 1)

            def rows7():
                dve.wait_ge(pe_done, at("rows6"))
                dve.memset(gS[:, :, :], 0.0)
                dve.tensor_copy(gcols[:, :, :, :].rearrange("p a b c -> p (a b c)"), bank(4)[:, 0:24]).then_inc(dve_done, 1)

            def cv_add(c):
                i = chunks[c]["i"]
                dve.wait_ge(act_done, at("cv_mul", c))
                dst = (gq_, gk_, gv_)[i // 2]
                for s in (1, 2, 3):
                    for m in range(2):
                        d = dst[:, 2 * (i % 2) + m, s:T]
                        ins = dve.scalar_tensor_tensor(d, bank(chunks[c]["banks"][0])[:, m * T:(m + 1) * T - s],
                                                       pcolumn("gdn_conv", (3 - s) * 12 + 2 * i + m), d, ALU.mult, ALU.add)
                    if s < 3:
                        link(ins)
                ins.then_inc(dve_done, 1)

            def hn_mul(job):
                dst, sq, rr, b, g, inv, f, gate = HN[job]
                dve.wait_ge(act_done, at("hn_r", job))
                ins = dve.scalar_tensor_tensor(dst, dst, g if g is not None else f, mat(rr), ALU.mult, ALU.mult)
                if gate is not None:
                    dve.wait_ge(act_done, at("copy", chunk_of("gz", 1)))
                    link(ins)
                    ins = dve.tensor_tensor(dst, dst, gate, ALU.mult)
                ins.then_inc(dve_done, 1)

            def g_mask(t):
                dve.wait_ge(pe_done, at("g_dec", t))
                for b, dst, m in ((4, gM, gda), (5, gAT, gdat)):
                    ins = dve.tensor_tensor(dst[:, :, :], per_head(bank(b)), m[:, :].unsqueeze(1).to_broadcast([P, NH, P]), ALU.add)
                ins.then_inc(dve_done, 1)

            def g_m(t):
                dve.wait_ge(pe_done, at("g_kk", t))
                dve.wait_ge(act_done, at("g_exp", t))
                dve.wait_ge(dve_done, at("rows7"))
                dve.tensor_tensor(gAT[:, :, :], per_head(bank(5)), gAT[:, :, :], ALU.mult)
                link(dve.tensor_tensor(gM[:, :, :], per_head(bank(4)), gM[:, :, :], ALU.mult))
                for h in range(NH):
                    ins = dve.scalar_tensor_tensor(gM[:, h, :], gM[:, h, :], gcols[:, t, 0, h:h + 1], strict[:, :], ALU.mult, ALU.mult)
                ins.then_inc(dve_done, 1)

            def g_vb(t):
                dve.wait_ge(pe_done, at("g_turn", t))
                for h in range(NH):
                    ins = dve.tensor_scalar(gVb[:, h, :], bank(5)[:, h * P:(h + 1) * P], gcols[:, t, 0, h:h + 1], None, ALU.mult)
                ins.then_inc(dve_done, 1)

            def l_upd(t, l):
                dve.wait_ge(pool_done, at("l_mask", t, l))
                if l == 0:
                    dve.wait_ge(pe_done, at("l_u", t, 0))
                    dve.tensor_tensor(gX[:, :, :], gX[:, :, :], gMs[0][:, :, :], ALU.subtract)
                else:
                    dve.wait_ge(pe_done, at("l_x", t, l))
                    if l < 5:
                        dve.tensor_tensor(gX[:, :, :], gX[:, :, :], per_head(bank(5)), ALU.subtract)
                dve.tensor_tensor(gY[:, :, :], gY[:, :, :], per_head(bank(4)), ALU.subtract).then_inc(dve_done, 1)

            def g_u(t):
                dve.wait_ge(pe_done, at("g_uw", t))
                dve.wait_ge(pool_done, at("l_mask", t, 5))
                dve.tensor_copy(gM[:, :, :], per_head(bank(4))).then_inc(dve_done, 1)

            def g_qg(t):
                dve.wait_ge(act_done, at("g_egc", t))
                s = slice(t * P, (t + 1) * P)
                dve.tensor_tensor(gq_[:, :, s], gq_[:, :, s], gX[:, :, :], ALU.mult).then_inc(dve_done, 1)

            def r_vn(t, j):
                r = slice(j * CH, (j + 1) * CH)
                dve.wait_ge(pe_done, at("r_ws", t, j))
                dve.tensor_tensor(gMs0[r, :, :], gM[r, :, :], per_head(banks[r, 4, :]), ALU.subtract).then_inc(dve_done, 1)

            def r_s(t, j):
                dve.wait_ge(pe_done, at("r_o", t, j))
                last = (j + 1) * CH - 1
                for h in range(NH):
                    ins = dve.scalar_tensor_tensor(gS[:, h, :], gS[:, h, :], gX[:, h, last:last + 1], bank(4)[:, h * P:(h + 1) * P],
                                                   ALU.mult, ALU.add)
                ins.then_inc(dve_done, 1)

            def sm(kind, h):
                s_, pt_, b, b2, nm, rs, rc = lane(kind, h)
                dve.wait_ge(pe_done, at("sc", kind, h))
                if before(kind, h) is not None:
                    dve.wait_ge(pe_done, at("pt", kind, before(kind, h)))
                v = bank(b).rearrange("p (t k) -> p t k", t=NT)
                if kind == "fox":
                    link(dve.tensor_tensor(mat(s_), v, cmask[:, :, :], ALU.add))
                    v = mat(s_)
                elif kind == "moba":
                    dve.wait_ge(pool_done, at("pool_tables"))
                    link(dve.scalar_tensor_tensor(mat(s_), dist[:, :, :], -SLOPE[h] / FACTOR[kind], v, ALU.mult, ALU.add))
                    v = mat(s_)
                ins = dve.tensor_reduce(nm, v, AX_X, ALU.max, negate=True)
                if FACTOR[kind] != 1.0:
                    link(ins)
                    ins = dve.tensor_scalar(nm, nm, FACTOR[kind], None, ALU.mult)
                ins.then_inc(dve_done, 1)

            def pn(kind, h):
                s_, pt_, b, b2, nm, rs, rc = lane(kind, h)
                dve.wait_ge(act_done, at("ex", kind, h))
                link(dve.reciprocal(rc, rs))
                for t in range(NT):
                    ins = dve.tensor_scalar(s_[:, t * T:(t + 1) * T], s_[:, t * T:(t + 1) * T], rc[:, t:t + 1], None, ALU.mult)
                ins.then_inc(dve_done, 1)

            def ol(kind, h):
                s_, pt_, b, *_ = lane(kind, h)
                dve.wait_ge(act_done, at("oc", kind, h))
                if kind == "mem":
                    o, i, hi_ = y2l[:, h, :], bank(b)[:, 0:T], y2h[:, h, :]
                elif kind == "moba":
                    r = slice(64 * (h % 2), 64 * (h % 2) + 64)
                    o, i, hi_ = y5l[r, h // 2, :], banks[r, b, 0:T], y5h[r, h // 2, :]
                else:
                    o, i, hi_ = y5l[:, 2 * h:2 * h + 2, :], bank(b).rearrange("p (a b) -> p a b", a=2), y5h[:, 2 * h:2 * h + 2, :]
                dve.tensor_tensor(o, i, hi_, ALU.subtract).then_inc(dve_done, 1)

            def z_lk(h):
                dve.wait_ge(act_done, at("z_e", h))
                n = T + P
                if h:
                    dve.wait_ge(pe_done, at("z_rc", h - 1))
                link(dve.scalar_tensor_tensor(PT1[:, 0:n], S1[:, 0:n], 0.0, PT1[:, 0:n], ALU.max, ALU.add))
                link(dve.tensor_scalar(PT1[:, 0:n], PT1[:, 0:n], -1.0, None, ALU.mult))
                for o in (0, T):
                    ins = dve.tensor_tensor(PT1[:, o:o + P], PT1[:, o:o + P], sbm[:, :], ALU.mult)
                ins.then_inc(dve_done, 1)

            def z_w(h):
                dve.wait_ge(pe_done, at("z_rc", h))
                n = T + P
                link(dve.tensor_tensor(S1[:, 0:n], S1[:, 0:n], bank(7)[:, 0:n], ALU.add))
                for o in (0, T):
                    ins = dve.tensor_tensor(S1[:, o:o + P], S1[:, o:o + P], sba[:, :], ALU.add)
                ins.then_inc(dve_done, 1)

            def yl_(br):
                dve.wait_ge(act_done, at("yh", br))
                dve.tensor_tensor(ybl[br][:, :, :], (fq_, gq_, sq_)[br][:, :, :], ybh[br][:, :, :], ALU.subtract).then_inc(dve_done, 1)

            def gated(c):
                ch = chunks[c]
                dve.wait_ge(pe_done, at("mm", c, 1))
                dve.wait_ge(act_done, at("gsig", ch["br"]))
                for q in range(2):
                    g = gates[:, 8 * ch["br"] + 4 * ch["i"] + 2 * q:8 * ch["br"] + 4 * ch["i"] + 2 * q + 2, :]
                    ins = dve.tensor_tensor(g, g, bank(ch["banks"][q]).rearrange("p (a b) -> p a b", a=2), ALU.mult)
                ins.then_inc(dve_done, 1)

            def premix():
                g = [gates[:, 8 * br:8 * br + 8, :] for br in BRANCHES[:2]]
                dve.tensor_tensor(g[0], g[0], g[1], ALU.add).then_inc(dve_done, 1)

            def mix(q):
                g = [gates[:, 8 * br + 2 * q:8 * br + 2 * q + 2, :] for br in (0, BRANCHES[0], BRANCHES[2])]
                dve.tensor_tensor(g[0], g[1], g[2], ALU.add).then_inc(dve_done, 1)

            def mixl(q):
                dve.wait_ge(act_done, at("mixh", q))
                dve.tensor_tensor(xl[:, 2 * q:2 * q + 2, :], gates[:, 2 * q:2 * q + 2, :], xh[:, 2 * q:2 * q + 2, :],
                                  ALU.subtract).then_inc(dve_done, 1)

            def resid(c, t):
                dve.wait_ge(pe_done, at("mm", c, 1))
                dve.tensor_tensor(x[:, t, :], x[:, t, :], banks[:, 4 + 2 * t:6 + 2 * t, :].rearrange("p a b -> p (a b)"),
                                  ALU.add).then_inc(dve_done, 1)

            def post0(c, t):
                dve.wait_ge(pe_done, at("mm", c, 1))
                if t == 0:
                    dve.wait_ge(act_done, at("post1", c, 0))
                dve.wait_ge(pe_done, at("nt", LAST_NORM[c], 3))
                dve.wait_ge(gains_in, 16 * (POSTS.index(c) + 1))
                f = 0.5 if chunks[c]["name"] in ("ffn1_w_down_2", "ffn2_w_down_2") else 1.0
                dve.scalar_tensor_tensor(xs[:, t, :], banks[:, 4 + 2 * t:6 + 2 * t, :].rearrange("p a b -> p (a b)"),
                                         f, gain[:, :], ALU.mult, ALU.mult).then_inc(dve_done, 1)

            def post2(c, t):
                dve.wait_ge(act_done, at("post_r", c))
                dve.scalar_tensor_tensor(x[:, t, :], xs[:, t, :], rn[:, t:t + 1], x[:, t, :], ALU.mult, ALU.add).then_inc(dve_done, 1)

            def cd(i):
                dve.wait_ge(act_done, at("ca", i))
                for s in (1, 2):
                    for a, c in enumerate(pair(0, i)):
                        for m in range(2):
                            d = CA[i % 2][:, a, m * T + s:(m + 1) * T]
                            ins = dve.scalar_tensor_tensor(d, bank(chunks[c]["banks"][0])[:, m * T:(m + 1) * T - s],
                                                           pcolumn("ffn_conv", (2 - s) * 2 * KF + a * KF + 2 * i + m), d,
                                                           ALU.mult, ALU.add)
                    if s == 1:
                        link(ins)
                ins.then_inc(dve_done, 1)

            def fm(f, i):
                dve.wait_ge(act_done, at("fs", f, i))
                if f == 0:
                    other = CA[i % 2][:, 1, :]
                else:
                    other = bank(chunks[pair(f, i)[1]]["banks"][0])
                    dve.wait_ge(pe_done, at("mm", pair(f, i)[1], 1))
                dve.tensor_tensor(SG[i % 2][:, :], SG[i % 2][:, :], other, ALU.mult).then_inc(dve_done, 1)

            def fl(f, i):
                dve.wait_ge(act_done, at("fh", f, i))
                dve.tensor_tensor(hl[:, 2 * i:2 * i + 2, :], mat(SG[i % 2]), hh[:, 2 * i:2 * i + 2, :], ALU.subtract).then_inc(dve_done, 1)

            def pl_win(g):
                dve.wait_ge(act_done, at("copy", chunk_of("pin", 1)))
                dve.wait_ge(pool_done, at("pool_tables"))
                cur = pin[:, g, :]
                if g == 0:
                    link(dve.reciprocal(rcnt[:, :, 0:16], rcnt[:, :, 0:16]))
                for l in range(g + 1):
                    s, nxt = 1 << l, win[:, l % 2, :]
                    dve.tensor_copy(nxt[:, 0:s], cur[:, 0:s])
                    link(dve.tensor_tensor(nxt[:, s:T], cur[:, s:T], cur[:, 0:T - s], ALU.add))
                    cur = nxt
                link(dve.tensor_tensor(cur, cur, rcnt[:, g, :], ALU.mult))
                dve.tensor_tensor(pin[:, g, :], cur, pin[:, g, :], ALU.subtract).then_inc(dve_done, 1)

            def pl_l(g):
                dve.wait_ge(act_done, at("pl_h", g))
                dve.scalar_tensor_tensor(y5l[:, 4 + g, :], bank(4 + g)[:, 0:T], pcolumn("pool_scale_2", g), y5h[:, 4 + g, :],
                                         ALU.mult, ALU.subtract).then_inc(dve_done, 1)

            steps = dict(locals())
            steps["yl"] = yl_
            run(dve, "dve", steps)


def kernel(**inputs):
    import concourse.bacc as bacc
    from concourse.bass_utils import run_bass_kernel_spmd

    nc = bacc.Bacc("TRN2", target_bir_lowering=False, num_devices=1)
    flat = {name: np.asarray(a).reshape(-1, np.shape(a)[-1]) for name, a in inputs.items()}
    col, _, n = param_columns()
    packed = np.zeros((3 * P, P), np.float32)
    for name, r in col.items():
        rows = flat.pop(name).reshape(-1, P)
        packed[r:r + len(rows)] = rows
    flat["params"] = packed
    flat["gate_params"] = np.stack([flat.pop(k)[0] for k in ("fox_fbias", "gdn_a_log", "gdn_dt_bias")], axis=1)
    arrays, w = {}, {}
    for name, a in flat.items():
        a = np.ascontiguousarray(a)
        arrays[f"in_{name}"] = a
        w[name] = nc.dram_tensor(f"in_{name}", a.shape, mybir.dt.from_np(a.dtype), kind="ExternalInput").ap()
    out = nc.dram_tensor("out", (T, D), F32, kind="ExternalOutput").ap()
    two_blocks_kernel(nc, w, out)
    r = run_bass_kernel_spmd(nc, [arrays], core_ids=[0])
    return r.results[0]["out"].reshape(1, T, D)
```
